# Optimizing a Trainium2 kernel written in Bass

```python
import math
import jax, jax.numpy as jnp
from jax import lax
import numpy as np

D_MODEL = 1024
BATCH = 1
SEQ = 1024
DEPTH = 1

EPS = 1e-6
D_FF = 2816
FFN_RES_WEIGHT = 0.5
N_MOD = 9

SWA_HEADS = 8
SWA_KV_HEADS = 2
SWA_HEAD_DIM = 64
SWA_GROUP = SWA_HEADS // SWA_KV_HEADS
WINDOW = 128

MLA_HEADS = 4
MLA_Q_RANK = 256
MLA_KV_RANK = 128
MLA_NOPE = 128
MLA_ROPE = 64
MLA_V = 128
ROPE_THETA = 10000.0
Q_BLOCK = 128

NUM_BUCKETS = 32
MAX_DISTANCE = 128

IN_SPLITS = (SWA_HEADS * SWA_HEAD_DIM, SWA_KV_HEADS * SWA_HEAD_DIM, SWA_KV_HEADS * SWA_HEAD_DIM,
             MLA_Q_RANK, MLA_KV_RANK, MLA_ROPE)
D_IN = sum(IN_SPLITS)
MIX_OUT = SWA_HEADS * SWA_HEAD_DIM + MLA_HEADS * MLA_V

kernel_name = "hybrid_swa_sink_mla_macaron_adaln"

def rms_norm(x, g):
    xf = x.astype(jnp.float32)
    y = xf * lax.rsqrt(jnp.mean(xf * xf, axis=-1, keepdims=True) + EPS)
    return (y * g.astype(jnp.float32)).astype(x.dtype)

def modulate(h, shift, scale):
    return h * (1 + scale[:, None, :]) + shift[:, None, :]

def swiglu(h, w_gate, w_up, w_down):
    return (jax.nn.silu(h @ w_gate) * (h @ w_up)) @ w_down

def t5_bucket(dist):
    max_exact = NUM_BUCKETS // 2
    n = jnp.maximum(dist, 0)
    nf = jnp.maximum(n, 1).astype(jnp.float32)
    large = max_exact + (jnp.log(nf / max_exact) / math.log(MAX_DISTANCE / max_exact)
                         * (NUM_BUCKETS - max_exact)).astype(jnp.int32)
    large = jnp.minimum(large, NUM_BUCKETS - 1)
    return jnp.where(n < max_exact, n, large)

def rope_tables(seq, dim):
    inv = ROPE_THETA ** (-jnp.arange(0, dim, 2, dtype=jnp.float32) / dim)
    ang = jnp.arange(seq, dtype=jnp.float32)[:, None] * inv[None, :]
    return jnp.cos(ang), jnp.sin(ang)

def apply_rope(x, cos, sin):
    c = cos[None, :, None, :].astype(x.dtype)
    s = sin[None, :, None, :].astype(x.dtype)
    x1, x2 = jnp.split(x, 2, axis=-1)
    return jnp.concatenate([x1 * c - x2 * s, x2 * c + x1 * s], axis=-1)

def sliding_window_gqa(q, k, v, sinks, rel_bias):
    B, S = q.shape[0], q.shape[1]
    nb = S // WINDOW
    qb = q.reshape(B, nb, WINDOW, SWA_KV_HEADS, SWA_GROUP, SWA_HEAD_DIM)
    kb = k.reshape(B, nb, WINDOW, SWA_KV_HEADS, SWA_HEAD_DIM)
    vb = v.reshape(B, nb, WINDOW, SWA_KV_HEADS, SWA_HEAD_DIM)
    pad_k = jnp.zeros_like(kb[:, :1])
    kk = jnp.concatenate([jnp.concatenate([pad_k, kb[:, :-1]], axis=1), kb], axis=2)
    vv = jnp.concatenate([jnp.concatenate([jnp.zeros_like(vb[:, :1]), vb[:, :-1]], axis=1), vb], axis=2)

    s = jnp.einsum('bnqhgd,bnkhd->bnhgqk', qb, kk).astype(jnp.float32) * (SWA_HEAD_DIM ** -0.5)

    qi = jnp.arange(WINDOW)[:, None]
    kj = jnp.arange(2 * WINDOW)[None, :]
    dist = qi + WINDOW - kj
    band = (dist >= 0) & (dist < WINDOW)
    blk = jnp.arange(nb)[:, None]
    key_ok = (blk > 0) | (jnp.arange(2 * WINDOW)[None, :] >= WINDOW)
    valid = band[None, :, :] & key_ok[:, None, :]

    bias = rel_bias.astype(jnp.float32)[t5_bucket(dist)]
    bias = bias.transpose(2, 0, 1).reshape(SWA_KV_HEADS, SWA_GROUP, WINDOW, 2 * WINDOW)
    s = jnp.where(valid[None, :, None, None], s + bias[None, None], -jnp.inf)

    sink = jnp.broadcast_to(sinks.astype(jnp.float32).reshape(1, 1, SWA_KV_HEADS, SWA_GROUP, 1, 1),
                            s.shape[:-1] + (1,))
    p = jax.nn.softmax(jnp.concatenate([s, sink], axis=-1), axis=-1)[..., :-1]
    o = jnp.einsum('bnhgqk,bnkhd->bnqhgd', p.astype(vv.dtype), vv)
    return o.reshape(B, S, SWA_HEADS * SWA_HEAD_DIM)

def mla_attention(q_lat, kv_lat, k_rope, q_norm, kv_norm, w_uq, w_ukv):
    B, S = q_lat.shape[0], q_lat.shape[1]
    cos, sin = rope_tables(S, MLA_ROPE)
    q = (rms_norm(q_lat, q_norm) @ w_uq).reshape(B, S, MLA_HEADS, MLA_NOPE + MLA_ROPE)
    q_nope, q_rope = q[..., :MLA_NOPE], apply_rope(q[..., MLA_NOPE:], cos, sin)
    kv = (rms_norm(kv_lat, kv_norm) @ w_ukv).reshape(B, S, MLA_HEADS, MLA_NOPE + MLA_V)
    k_nope, v = kv[..., :MLA_NOPE], kv[..., MLA_NOPE:]
    k_r = apply_rope(k_rope[:, :, None, :], cos, sin)[:, :, 0, :]
    scale = (MLA_NOPE + MLA_ROPE) ** -0.5

    nb = S // Q_BLOCK
    qn = q_nope.reshape(B, nb, Q_BLOCK, MLA_HEADS, MLA_NOPE).transpose(1, 0, 2, 3, 4)
    qr = q_rope.reshape(B, nb, Q_BLOCK, MLA_HEADS, MLA_ROPE).transpose(1, 0, 2, 3, 4)
    kpos = jnp.arange(S)

    def one_block(args):
        qn_b, qr_b, i = args
        s = (jnp.einsum('bqhd,bkhd->bhqk', qn_b, k_nope)
             + jnp.einsum('bqhd,bkd->bhqk', qr_b, k_r)).astype(jnp.float32) * scale
        qpos = i * Q_BLOCK + jnp.arange(Q_BLOCK)
        s = jnp.where(kpos[None, :] <= qpos[:, None], s, -jnp.inf)
        p = jax.nn.softmax(s, axis=-1).astype(v.dtype)
        return jnp.einsum('bhqk,bkhd->bqhd', p, v)

    o = lax.map(one_block, (qn, qr, jnp.arange(nb)))
    return o.transpose(1, 0, 2, 3, 4).reshape(B, S, MLA_HEADS * MLA_V)

def token_mixing(h, w_in, q_norm, kv_norm, w_uq, w_ukv, sinks, w_o, rel_bias):
    B, S = h.shape[0], h.shape[1]
    proj = h @ w_in
    idx = np.cumsum(IN_SPLITS)[:-1].tolist()
    q_a, k_a, v_a, q_lat, kv_lat, k_rope = jnp.split(proj, idx, axis=-1)
    out_a = sliding_window_gqa(q_a.reshape(B, S, SWA_HEADS, SWA_HEAD_DIM),
                               k_a.reshape(B, S, SWA_KV_HEADS, SWA_HEAD_DIM),
                               v_a.reshape(B, S, SWA_KV_HEADS, SWA_HEAD_DIM),
                               sinks, rel_bias)
    out_b = mla_attention(q_lat, kv_lat, k_rope, q_norm, kv_norm, w_uq, w_ukv)
    return jnp.concatenate([out_a, out_b], axis=-1) @ w_o

def setup_inputs(seed: int = 0) -> dict:
    key = jax.random.key(seed)
    ks = jax.random.split(key, 24)
    L, D = DEPTH, D_MODEL

    def w(k, shape, fan_in):
        return jax.random.normal(k, shape, jnp.float32) * fan_in ** -0.5

    def gain(k, shape):
        return 1.0 + 0.05 * jax.random.normal(k, shape, jnp.float32)

    return {
        "x": jax.random.normal(ks[0], (BATCH, SEQ, D), jnp.float32),
        "c": jax.random.normal(ks[1], (BATCH, D), jnp.float32),
        "w_mod": w(ks[2], (L, D, N_MOD * D), D) * 0.5,
        "b_mod": 0.02 * jax.random.normal(ks[3], (L, N_MOD * D), jnp.float32),
        "norm_ffn1": gain(ks[4], (L, D)),
        "ffn1_gate": w(ks[5], (L, D, D_FF), D),
        "ffn1_up": w(ks[6], (L, D, D_FF), D),
        "ffn1_down": w(ks[7], (L, D_FF, D), D_FF),
        "norm_mix": gain(ks[8], (L, D)),
        "w_in": w(ks[9], (L, D, D_IN), D),
        "q_norm": gain(ks[10], (L, MLA_Q_RANK)),
        "kv_norm": gain(ks[11], (L, MLA_KV_RANK)),
        "w_uq": w(ks[12], (L, MLA_Q_RANK, MLA_HEADS * (MLA_NOPE + MLA_ROPE)), MLA_Q_RANK),
        "w_ukv": w(ks[13], (L, MLA_KV_RANK, MLA_HEADS * (MLA_NOPE + MLA_V)), MLA_KV_RANK),
        "sinks": 0.5 * jax.random.normal(ks[14], (L, SWA_HEADS), jnp.float32),
        "w_o": w(ks[15], (L, MIX_OUT, D), MIX_OUT),
        "norm_ffn2": gain(ks[16], (L, D)),
        "ffn2_gate": w(ks[17], (L, D, D_FF), D),
        "ffn2_up": w(ks[18], (L, D, D_FF), D),
        "ffn2_down": w(ks[19], (L, D_FF, D), D_FF),
        "rel_bias": 0.5 * jax.random.normal(ks[20], (NUM_BUCKETS, SWA_HEADS), jnp.float32),
        "norm_final": gain(ks[21], (D,)),
    }

def reference(x, c, w_mod, b_mod, norm_ffn1, ffn1_gate, ffn1_up, ffn1_down, norm_mix, w_in,
              q_norm, kv_norm, w_uq, w_ukv, sinks, w_o, norm_ffn2, ffn2_gate, ffn2_up, ffn2_down,
              rel_bias, norm_final):
    c_act = jax.nn.silu(c)
    for l in range(DEPTH):
        mod = c_act @ w_mod[l] + b_mod[l]
        sh1, sc1, g1, sh2, sc2, g2, sh3, sc3, g3 = jnp.split(mod, N_MOD, axis=-1)

        h = modulate(rms_norm(x, norm_ffn1[l]), sh1, sc1)
        x = x + FFN_RES_WEIGHT * g1[:, None, :] * swiglu(h, ffn1_gate[l], ffn1_up[l], ffn1_down[l])

        h = modulate(rms_norm(x, norm_mix[l]), sh2, sc2)
        x = x + g2[:, None, :] * token_mixing(h, w_in[l], q_norm[l], kv_norm[l], w_uq[l], w_ukv[l],
                                              sinks[l], w_o[l], rel_bias)

        h = modulate(rms_norm(x, norm_ffn2[l]), sh3, sc3)
        x = x + FFN_RES_WEIGHT * g3[:, None, :] * swiglu(h, ffn2_gate[l], ffn2_up[l], ffn2_down[l])
    return rms_norm(x, norm_final)


_drawn_inputs = setup_inputs


def setup_inputs(seed=0):
    import zlib

    import numpy as np

    out = dict(_drawn_inputs(seed))
    spreads = {}
    factors = {'b_mod': 3.706,
     'norm_ffn1': 7.72,
     'norm_mix': 8.0,
     'q_norm': 8.0,
     'kv_norm': 8.0,
     'sinks': 200.0,
     'norm_ffn2': 7.786,
     'rel_bias': 3.301}
    for name, (base, spread) in spreads.items():
        noise = np.random.default_rng([zlib.crc32(name.encode()), seed]).standard_normal(out[name].shape)
        drawn = base * np.exp(spread * noise) if base else spread * noise
        out[name] = __import__('jax').numpy.asarray(drawn.astype(out[name].dtype))
    for name, factor in factors.items():
        out[name] = (out[name] * factor).astype(out[name].dtype)
    return out
```

```python
from contextlib import ExitStack

import concourse.bass as bass
from concourse import mybir
from concourse.alu_op_type import AluOpType as ALU

F32 = mybir.dt.float32
F32R = mybir.dt.float32r
ACT = mybir.ActivationFunctionType
AX = mybir.AxisListType

P = 128
D = 1024
T = 1024
KC = D // P
HALF = 512
NH2 = T // HALF
D_FF = 2816
FPI = 2
ITERS = D_FF // P // FPI
N_MOD = 9
MODC = N_MOD * KC
EPS = 1e-6

SWA_HEADS = 8
SWA_GROUP = 4
SWA_DIM = 64
MLA_HEADS = 4
NOPE = 128
ROPE = 64
Q_RANK = 256
KV_RANK = 128
NBLK = T // P
BUCKETS = 32
LINE = 384
MLA_SCALE = (NOPE + ROPE) ** -0.5
SWA_SCALE = SWA_DIM ** -0.5

CPI = 3 * FPI
W_FFN = [0, CPI * ITERS + 21]
W_IN = CPI * ITERS
N_IN = 10
W_UQ = W_IN + N_IN
W_UKV = W_UQ + 2
W_OUT = W_UKV + 1
N_CHUNKS = 2 * CPI * ITERS + 21
RAW, SPLIT = 3, 6

NORM_AT = [0, 16, 38, 54]
LAT_AT = 32
STD_AT = [0, 2, 8, 10]
LAT_STD_AT = 4
X_AT = [0, 16 * ITERS + 16]
X_MIX = 16 * ITERS
MLA_FIRST = 2 * N_IN
SMALL = MODC + 4 * KC + 3


def units():
    mla = [("mla", h, i) for i in range(NBLK) for h in range(MLA_HEADS)]
    swa = [("swa", g, i) for i in range(NBLK) for g in range(2)]
    out = []
    for n in range(16):
        out += [mla[n], swa[n], mla[31 - n]]
    return out


def mixer_tiles():
    out = []
    for m in range(N_IN):
        out += [("in", m, h) for h in range(NH2)]
    out += [("knope", hd, h) for hd in range(MLA_HEADS) for h in range(NH2)]
    out += [("v", 0, b) for b in range(NBLK)]
    out += [("qnope", hd, h) for hd in range(MLA_HEADS) for h in range(NH2)]
    for r in range(2):
        for h in range(NH2):
            out += [("rope", r, h), ("swapped", r, h)]
    return out


KV, Q0, Q1, KROPE, KA, VA, QA = 0, 1, 2, 3, 4, 5, 6
TILES = mixer_tiles()


def by_vector(p):
    what, m, _ = TILES[p]
    return what in ("v", "rope", "swapped") or (what == "in" and m == KROPE)


def evacuated(p):
    mine = by_vector(p)
    return mine, sum(by_vector(q) == mine for q in range(p + 1))


def build(nc, xT, c_in, w_modT, small_in, wstream, const_in, tab_in, sinks_in, rel_in, oh_in, lm_in,
          out):
    ctx = ExitStack()
    with ctx:
        at = [4224]

        def sb(name, shape, dt, offset=None):
            size = 4
            for s in shape[1:]:
                size *= s
            if offset is None:
                offset = at[0]
                at[0] += (size + 31) // 32 * 32
            return nc.alloc_sbuf_tensor_at(name, shape, dt, offset=offset)

        x = sb("x", [P, KC, T], F32)
        h_at = at[0]
        h_hi = sb("h_hi", [P, KC, T], F32R)
        h_lo = sb("h_lo", [P, KC, T], F32R)
        w_raw = sb("w_raw", [P, RAW, D], F32)
        w_hi = sb("w_hi", [P, SPLIT, D], F32R)
        w_lo = sb("w_lo", [P, SPLIT, D], F32R)
        s_at = at[0]
        u_hi = sb("u_hi", [P, FPI, T], F32R)
        u_lo = sb("u_lo", [P, FPI, T], F32R)
        sil = sb("sil", [P, NH2, HALF], F32)
        uf = sb("uf", [P, NH2, HALF], F32)
        mod_raw = sb("mod_raw", [P, 4, D], F32)
        c_act = sb("c_act", [P, D], F32)
        tt = sb("tt", [P, 2, HALF], F32)
        sq = sb("sq", [P, 2, HALF], F32)
        std = sb("std", [P, 2, HALF], F32)
        rstd = sb("rstd", [P, 2, HALF], F32)
        small = sb("small", [P, SMALL], F32)
        consts = sb("consts", [P, 3, P], F32)
        mod = sb("mod", [P, MODC], F32)
        mod_acc = sb("mod_acc", [P, 4], F32)
        scale_v = sb("scale_v", [P, 3, KC], F32)
        gate_v = sb("gate_v", [P, 3, KC], F32)
        sinks = sb("sinks", [P, SWA_HEADS], F32)
        mx = sb("mx", [P, 2, 4], F32)
        negm = sb("negm", [P, 2, 4], F32)
        dsink = sb("dsink", [P, 2, 4], F32)
        esink = sb("esink", [P, 2, 4], F32)
        den = sb("den", [P, 2, 4], F32)
        rden = sb("rden", [P, 2, 4], F32)
        eps = sb("eps", [P, 1], F32)
        o_all = sb("o_all", [P, KC, T], F32, s_at)
        kvl = sb("kvl", [P, T], F32, s_at + 16384)
        ql = sb("ql", [P, 2, T], F32, s_at + 20480)
        vT = sb("vT", [P, T], F32, s_at + 28672)
        k_a = sb("k_a", [P, T], F32, s_at + 32768)
        v_a = sb("v_a", [P, NBLK, P], F32, s_at + 36864)
        k_r = sb("k_r", [P, T], F32, s_at + 40960)
        x_at = h_at - 32768
        q_hi = sb("q_hi", [P, 2, T], F32R, x_at)
        q_lo = sb("q_lo", [P, 2, T], F32R, x_at + 8192)
        kv_hi = sb("kv_hi", [P, T], F32R, x_at + 16384)
        kv_lo = sb("kv_lo", [P, T], F32R, x_at + 20480)
        tab = sb("tab", [P, 2, T], F32, x_at + 24576)
        k_nope = sb("k_nope", [P, MLA_HEADS, T], F32, h_at)
        v_b = sb("v_b", [P, NBLK, MLA_HEADS * P], F32, h_at + 16384)
        q_r = sb("q_r", [P, 2, T], F32, h_at + 32768)
        p_sb = sb("p_sb", [P, 2, D], F32, h_at + 40960)
        pt_sb = sb("pt_sb", [P, 2, D], F32, h_at + 49152)
        bias = sb("bias", [P, SWA_HEADS, 2 * P], F32, h_at + 57344)
        onehot = sb("onehot", [BUCKETS, LINE], F32, h_at + 40960)
        linemask = sb("linemask", [SWA_HEADS, LINE], F32, h_at + 40960 + 1536)
        line = sb("line", [SWA_HEADS, LINE], F32, h_at + 40960 + 3072)
        rel = sb("rel", [BUCKETS, SWA_HEADS], F32, h_at + 40960 + 4608)

        ident, mask, ones = (consts[:, j, :] for j in range(3))
        bmod = small[:, 0:MODC]

        def gain(s):
            return small[:, MODC + KC * s:MODC + KC * s + KC]

        lat_gain = small[:, MODC + 4 * KC:SMALL]

        ps = ctx.enter_context(nc.psum_tensor("ps", [P, 8, HALF], F32))

        x_save = nc.dram_tensor("x_save", [P, KC, T], F32).ap()
        line_dram = nc.dram_tensor("line_dram", [P, SWA_HEADS, LINE], F32)

        def sem(name):
            return ctx.enter_context(nc.semaphore(name))

        x_landed = [sem(f"x_landed{j}") for j in range(2)]
        c_landed = sem("c_landed")
        small_landed = sem("small_landed")
        const_landed = sem("const_landed")
        eps_ready = sem("eps_ready")
        sinks_landed = sem("sinks_landed")
        raw_landed = [sem(f"raw_landed{j}") for j in range(RAW)]
        hi_split = sem("hi_split")
        lo_split = sem("lo_split")
        mod_landed = [sem(f"mod_landed{j}") for j in range(4)]
        mod_used = sem("mod_used")
        mod_ready = sem("mod_ready")
        vec_ready = sem("vec_ready")
        c_ready = sem("c_ready")
        sq_done = sem("sq_done")
        stat_done = sem("stat_done")
        std_done = sem("std_done")
        rstd_done = sem("rstd_done")
        t_done = sem("t_done")
        n_hi = sem("n_hi")
        n_lo = sem("n_lo")
        gu_ready = sem("gu_ready")
        sil_done = sem("sil_done")
        uf_done = sem("uf_done")
        u_hi_done = sem("u_hi_done")
        u_lo_done = sem("u_lo_done")
        y_ready = sem("y_ready")
        x_added = sem("x_added")
        x_saved = sem("x_saved")
        tab_landed = sem("tab_landed")
        oh_landed = sem("oh_landed")
        rel_landed = sem("rel_landed")
        lm_landed = sem("lm_landed")
        line_ready = sem("line_ready")
        line_added = sem("line_added")
        line_saved = sem("line_saved")
        bias_landed = sem("bias_landed")
        x_back = sem("x_back")
        tile_ready = sem("tile_ready")
        act_emptied = sem("act_emptied")
        dve_emptied = sem("dve_emptied")
        rope_part = sem("rope_part")
        rope_done = sem("rope_done")
        vt_ready = sem("vt_ready")
        va_done = sem("va_done")
        s_ready = sem("s_ready")
        biased = sem("biased")
        max_part = sem("max_part")
        max_done = sem("max_done")
        exp_done = sem("exp_done")
        den_part = sem("den_part")
        p_done = sem("p_done")
        pt_ready = sem("pt_ready")
        pt_act = sem("pt_act")
        pt_dve = sem("pt_dve")
        o_ready = sem("o_ready")
        o_done = sem("o_done")
        o_hi = sem("o_hi")
        o_lo = sem("o_lo")
        out_ready = sem("out_ready")
        out_saved = sem("out_saved")

        def half(h):
            return slice(h * HALF, (h + 1) * HALF)

        def blk(i):
            return slice(i * P, (i + 1) * P)

        def slots(n):
            return n % RAW, n % SPLIT

        N_ACT = sum(not by_vector(p) for p in range(len(TILES)))
        N_DVE = len(TILES) - N_ACT
        UNITS = units()
        NU = len(UNITS)

        def pt_cols(u):
            kind, _, i = UNITS[u]
            return (i + 1) * P if kind == "mla" else SWA_GROUP * (P if i == 0 else 2 * P)

        block = ctx.enter_context(nc.Block())

        @block.sync
        def _(sp):
            for j in range(2):
                sp.dma_start(x[:, 4 * j:4 * j + 4, :], xT[:, 4 * j:4 * j + 4, :]).then_inc(x_landed[j], 16)
            for n in range(RAW):
                sp.dma_start(w_raw[:, n, :], wstream[n]).then_inc(raw_landed[n], 16)
            with nc.sync.Fori(1, N_CHUNKS // RAW) as g:
                for j in range(RAW):
                    sp.wait_ge(lo_split, g * RAW + (j - RAW + 1))
                    sp.dma_start(w_raw[:, j, :], wstream[bass.ds(g * RAW + j, 1), :, :].rearrange(
                        "a p d -> (a p) d")).then_inc(raw_landed[j], 16)
            for h in range(NH2):
                for c in range(0, KC, 2):
                    sp.wait_ge(out_ready, KC * h + c + 2)
                    sp.dma_start(out[:, c:c + 2, half(h)], x[:, c:c + 2, half(h)]).then_inc(out_saved, 16)
            sp.wait_ge(out_saved, 16 * KC)

        @block.gpsimd
        def _(pool):
            for j in range(4):
                pool.dma_start(mod_raw[:, j, :], w_modT[j]).then_inc(mod_landed[j], 16)
            with nc.gpsimd.Fori(1, MODC // 4) as g:
                for j in range(4):
                    pool.wait_ge(mod_used, g * 4 + (j - 3))
                    pool.dma_start(mod_raw[:, j, :], w_modT[bass.ds(g * 4 + j, 1), :, :].rearrange(
                        "a p d -> (a p) d")).then_inc(mod_landed[j], 16)
            pool.wait_ge(x_added, X_MIX)
            pool.dma_start(x_save, x[:]).then_inc(x_saved, 16)
            pool.wait_ge(x_saved, 16)
            pool.wait_ge(n_lo, LAT_AT)
            pool.dma_start(tab[:], tab_in).then_inc(tab_landed, 16)
            pool.wait_ge(tile_ready, 2 * N_IN)
            pool.dma_start(onehot[:], oh_in).then_inc(oh_landed, 16)
            pool.dma_start(rel[:], rel_in).then_inc(rel_landed, 16)
            pool.dma_start(linemask[:], lm_in).then_inc(lm_landed, 16)
            pool.wait_ge(line_added, 1)
            pool.dma_start(line_dram.ap().rearrange("q h t -> h q t"), line[:].rearrange(
                "h (q t) -> h q t", q=1).broadcast_to([SWA_HEADS, P, LINE])).then_inc(line_saved, 16)
            pool.wait_ge(line_saved, 16)
            pool.dma_start(bias[:], bass.AP(line_dram, P - 1, [[SWA_HEADS * LINE - 1, P], [LINE, SWA_HEADS],
                                                               [1, 2 * P]])).then_inc(bias_landed, 16)
            pool.wait_ge(tile_ready, len(TILES))
            pool.wait_ge(rope_done, 4)
            pool.dma_start(x[:], x_save).then_inc(x_back, 16)
            pool.wait_ge(x_back, 16)

        @block.tensor
        def _(pe):
            def product(psum, wh, wl, ah, al, start, stop):
                pe.matmul(psum, wh, al, start=start, stop=False)
                pe.matmul(psum, wl, ah, start=False, stop=False)
                return pe.matmul(psum, wh, ah, start=False, stop=stop)

            def stats(first, tiles, bank):
                for k in range(tiles):
                    pe.wait_ge(sq_done, first + k + 1)
                    pe.matmul(ps[:, bank, :], ones, sq[:, (first + k) % 2, :], start=(k == 0),
                              stop=(k == tiles - 1)).then_inc(stat_done, 1)

            def gate_up(z, i, f, h, new_input):
                n = 4 * ITERS * z + i * 4 + (2 * f + h)
                if not isinstance(n, int) or n >= 2:
                    pe.wait_ge(uf_done, n - 1)
                for j in range(2):
                    s = (W_FFN[z] + 2 * f + j) % SPLIT
                    if h == 0:
                        pe.wait_ge(lo_split, i * CPI + (W_FFN[z] + 2 * f + j + 1))
                    for k in range(KC):
                        if new_input and j == 0:
                            pe.wait_ge(n_lo, NORM_AT[2 * z] + KC * h + k + 1)
                        mm = product(ps[:, 2 * h + j, :], w_hi[:, s, blk(k)], w_lo[:, s, blk(k)],
                                     h_hi[:, k, half(h)], h_lo[:, k, half(h)], k == 0, k == KC - 1)
                mm.then_inc(gu_ready, 1)

            def down(z, i, h, d):
                n = X_AT[z] + i * 16 + (KC * h + d)
                if not isinstance(n, int) or n >= 4:
                    pe.wait_ge(x_added, n - 3)
                for f in range(FPI):
                    s = (W_FFN[z] + 2 * FPI + f) % SPLIT
                    mm = product(ps[:, 4 + d % 4, :], w_hi[:, s, blk(d)], w_lo[:, s, blk(d)],
                                 u_hi[:, f, half(h)], u_lo[:, f, half(h)], f == 0, f == FPI - 1)
                mm.then_inc(y_ready, 1)

            def ffn_step(z, i, first=False, last=False):
                for f in range(FPI):
                    for h in range(NH2):
                        gate_up(z, i, f, h, first and f == 0)
                pe.wait_ge(lo_split, i * CPI + (W_FFN[z] + CPI))
                for h in range(NH2):
                    pe.wait_ge(u_lo_done, 4 * ITERS * z + i * 4 + (3 + h))
                    for d in range(KC):
                        down(z, i, h, d)
                        if last and h == 1 and d == 3:
                            stats(NORM_AT[2 * z + 1], KC, 0)
                if last:
                    stats(NORM_AT[2 * z + 1] + KC, KC, 2)

            def ffn(z):
                ffn_step(z, 0, first=True)
                with nc.tensor.Fori(1, ITERS - 1) as i:
                    ffn_step(z, i)
                ffn_step(z, ITERS - 1, last=True)

            def free_bank(p):
                if p >= 4:
                    vector, n = evacuated(p - 4)
                    pe.wait_ge(dve_emptied if vector else act_emptied, n)

            def mixer_in():
                for m in range(N_IN):
                    s = (W_IN + m) % SPLIT
                    pe.wait_ge(lo_split, W_IN + m + 1)
                    for h in range(NH2):
                        p = 2 * m + h
                        free_bank(p)
                        for k in range(KC):
                            if m == 0:
                                pe.wait_ge(n_lo, NORM_AT[1] + KC * h + k + 1)
                            mm = product(ps[:, 4 + p % 4, :], w_hi[:, s, blk(k)], w_lo[:, s, blk(k)],
                                         h_hi[:, k, half(h)], h_lo[:, k, half(h)], k == 0, k == KC - 1)
                        mm.then_inc(tile_ready, 1)
                    if m == KA:
                        stats(LAT_AT, 1, 0)
                        stats(LAT_AT + 1, 1, 2)
                        stats(LAT_AT + 2, 2, 1)
                        stats(LAT_AT + 4, 2, 3)
                    if m == QA:
                        pe.wait_ge(act_emptied, evacuated(2 * VA + 1)[1])
                        pe.wait_ge(std_done, LAT_STD_AT + 4)
                        for b in range(NBLK):
                            tr = pe.transpose(ps[:, b // 4, blk(b % 4)], vT[:, blk(b)], ident)
                            if b % 4 == 3:
                                tr.then_inc(vt_ready, 1)

            def latent_products():
                s_kv = W_UKV % SPLIT
                s_q = [(W_UQ + k) % SPLIT for k in range(2)]
                pe.wait_ge(lo_split, W_UKV + 1)
                pe.wait_ge(n_lo, LAT_AT + 6)
                for p in range(MLA_FIRST, len(TILES)):
                    what, m, h = TILES[p]
                    free_bank(p)
                    out_p = ps[:, 4 + p % 4, :]
                    if what == "knope":
                        mm = product(out_p, w_hi[:, s_kv, blk(m)], w_lo[:, s_kv, blk(m)],
                                     kv_hi[:, half(h)], kv_lo[:, half(h)], True, True)
                    elif what == "v":
                        mm = product(out_p, kv_hi[:, blk(h)], kv_lo[:, blk(h)],
                                     w_hi[:, s_kv, HALF:D], w_lo[:, s_kv, HALF:D], True, True)
                    else:
                        col = {"qnope": m, "rope": 4 + m, "swapped": 6 + m}[what]
                        for k in range(2):
                            mm = product(out_p, w_hi[:, s_q[k], blk(col)], w_lo[:, s_q[k], blk(col)],
                                         q_hi[:, k, half(h)], q_lo[:, k, half(h)], k == 0, k == 1)
                    mm.then_inc(tile_ready, 1)
                pe.wait_ge(oh_landed, 16)
                pe.wait_ge(rel_landed, 16)
                pe.matmul(ps[0:SWA_HEADS, 2, 0:LINE], rel[:], onehot[:], start=True, stop=True
                          ).then_inc(line_ready, 1)

            def scores(u):
                kind, a, i = UNITS[u]
                if u >= 2:
                    if UNITS[u - 2][0] == "mla":
                        pe.wait_ge(exp_done, u - 1)
                    else:
                        pe.wait_ge(biased, sum(v[0] == "swa" for v in UNITS[:u - 1]))
                b0 = 2 * (u % 2)
                if kind == "mla":
                    r = ROPE * (a % 2)
                    for lo in range(0, (i + 1) * P, HALF):
                        hi = min(lo + HALF, (i + 1) * P)
                        bank = ps[:, b0 + lo // HALF, :]
                        pe.matmul(bank[:, 0:hi - lo], o_all[:, 4 + a, blk(i)], k_nope[:, a, lo:hi],
                                  start=True, stop=False)
                        mm = pe.matmul(bank[:, 0:hi - lo], q_r[r:r + ROPE, a // 2, blk(i)],
                                       k_r[r:r + ROPE, lo:hi], start=False, stop=(hi <= i * P))
                        if hi > i * P:
                            mm = pe.matmul(bank[:, i * P - lo:hi - lo], ident, mask, start=False, stop=True)
                else:
                    g = SWA_DIM * a
                    lo, w = max(i - 1, 0) * P, P if i == 0 else 2 * P
                    for c in range(SWA_GROUP):
                        bank = ps[:, b0 + c * w // HALF, :]
                        mm = pe.matmul(bank[:, c * w % HALF:c * w % HALF + w], o_all[g:g + SWA_DIM, c, blk(i)],
                                       k_a[g:g + SWA_DIM, lo:lo + w], start=True, stop=True)
                mm.then_inc(s_ready, 1)

            def turn(u):
                kind, _, i = UNITS[u]
                pe.wait_ge(p_done, u + 1)
                if u >= 1:
                    pe.wait_ge(pt_act, u)
                    pe.wait_ge(pt_dve, sum(pt_cols(v) > HALF for v in range(u)))
                if kind == "mla":
                    moves = [(j, j * P) for j in range(i + 1)]
                else:
                    kbs = 1 if i == 0 else 2
                    moves = [(kb * SWA_GROUP + c, (c * kbs + kb) * P)
                             for kb in range(kbs) for c in range(SWA_GROUP)]
                for j, lo in moves:
                    tr = pe.transpose(ps[:, 4 + j // 4, blk(j % 4)], p_sb[:, u % 2, lo:lo + P], ident)
                tr.then_inc(pt_ready, 1)

            def values(u):
                kind, a, i = UNITS[u]
                pe.wait_ge(pt_act, u + 1)
                pe.wait_ge(pt_dve, sum(pt_cols(v) > HALF for v in range(u + 1)))
                if u >= 2:
                    pe.wait_ge(o_done, u - 1)
                if kind == "mla":
                    for j in range(i + 1):
                        mm = pe.matmul(ps[:, 6 + u % 2, 0:P], v_b[:, j, blk(a)], pt_sb[:, u % 2, blk(j)],
                                       start=(j == 0), stop=(j == i))
                else:
                    g = SWA_DIM * a
                    keys = [0] if i == 0 else [i - 1, i]
                    for n, b in enumerate(keys):
                        mm = pe.matmul(ps[g:g + SWA_DIM, 6 + u % 2, :], v_a[:, b, g:g + SWA_DIM],
                                       pt_sb[:, u % 2, half(n)], start=(n == 0), stop=(n == len(keys) - 1))
                mm.then_inc(o_ready, 1)

            def attention():
                pe.wait_ge(act_emptied, N_ACT)
                pe.wait_ge(dve_emptied, N_DVE)
                pe.wait_ge(rope_done, 4)
                pe.wait_ge(va_done, 2)
                pe.wait_ge(line_added, 1)
                for u in range(NU + 2):
                    if u < NU:
                        scores(u)
                    if 1 <= u <= NU:
                        turn(u - 1)
                    if u >= 2:
                        values(u - 2)

            def mixer_out():
                for d in range(KC):
                    s = (W_OUT + d) % SPLIT
                    pe.wait_ge(lo_split, W_OUT + d + 1)
                    for h in range(NH2):
                        w = 2 * d + h
                        if w >= 4:
                            pe.wait_ge(x_added, X_MIX + w - 3)
                        for k in range(KC):
                            if d == 0:
                                pe.wait_ge(o_lo, KC * h + k + 1)
                            mm = product(ps[:, 4 + w % 4, :], w_hi[:, s, blk(k)], w_lo[:, s, blk(k)],
                                         h_hi[:, k, half(h)], h_lo[:, k, half(h)], k == 0, k == KC - 1)
                        mm.then_inc(y_ready, 1)
                stats(NORM_AT[2], KC, 0)
                stats(NORM_AT[2] + KC, KC, 2)

            pe.wait_ge(const_landed, 16)
            stats(NORM_AT[0], KC, 0)
            stats(NORM_AT[0] + KC, KC, 2)
            ffn(0)
            mixer_in()
            latent_products()
            attention()
            mixer_out()
            ffn(1)

        def chunk_free(n):
            m = n - W_IN
            if m < -2:
                return gu_ready, 4 * ITERS - (0 if m >= -4 else 2)
            if m < 0:
                return y_ready, X_MIX
            if m < N_IN:
                return tile_ready, 2 * m + 2
            if n < W_UKV:
                return tile_ready, len(TILES)
            if n == W_UKV:
                return tile_ready, MLA_FIRST + 16
            return y_ready, X_MIX + 2 * (n - W_OUT) + 2

        @block.scalar
        def _(act):
            def hi_part(base, i, k, free):
                act.wait_ge(raw_landed[(base + k) % RAW], i * (16 * CPI // RAW) + 16 * ((base + k) // RAW + 1))
                if free is not None:
                    act.wait_ge(*free)
                act.activation(w_hi[:, (base + k) % SPLIT, :], w_raw[:, (base + k) % RAW, :], ACT.Copy
                               ).then_inc(hi_split, 1)

            def hi_of(n):
                hi_part(n, 0, 0, chunk_free(n - SPLIT))

            def square(n, source, ready):
                if ready is not None:
                    act.wait_ge(*ready)
                if n >= 2:
                    act.wait_ge(stat_done, n - 1)
                act.activation(sq[:, n % 2, :], source, ACT.Square).then_inc(sq_done, 1)

            def deviation(n, tiles_done, bank, size):
                act.wait_ge(stat_done, tiles_done)
                if n >= 2:
                    act.wait_ge(rstd_done, n - 1)
                act.activation(std[:, n % 2, :], ps[:, bank, :], ACT.Sqrt, bias=eps[:, 0:1],
                               scale=1.0 / size).then_inc(std_done, 1)

            def shifted(s, h, c):
                n = NORM_AT[s] + KC * h + c
                act.wait_ge(t_done, n + 1)
                act.activation(h_hi[:, c, half(h)], tt[:, n % 2, :], ACT.Identity,
                               bias=mod[:, 3 * KC * s + c:3 * KC * s + c + 1]).then_inc(n_hi, 1)

            def norm(s, tile_at):
                for c in range(KC):
                    square(NORM_AT[s] + c, x[:, c, half(0)], tile_at(0, c))
                deviation(STD_AT[s], NORM_AT[s] + KC, 0, D)
                for c in range(KC):
                    if s < 3:
                        shifted(s, 0, c)
                    square(NORM_AT[s] + KC + c, x[:, c, half(1)], tile_at(1, c))
                deviation(STD_AT[s] + 1, NORM_AT[s] + 2 * KC, 2, D)
                if s < 3:
                    for c in range(KC):
                        shifted(s, 1, c)

            def first_norm():
                for h in range(NH2):
                    for c in range(KC):
                        square(KC * h + c, x[:, c, half(h)], (x_landed[c // 4], 16))
                    deviation(h, KC * h + KC, 2 * h, D)
                for h in range(NH2):
                    for c in range(KC):
                        shifted(0, h, c)

            def silu(z, i, f, h):
                n = 4 * ITERS * z + i * 4 + (2 * f + h)
                act.wait_ge(gu_ready, n + 1)
                if not isinstance(n, int) or n >= 2:
                    act.wait_ge(uf_done, n - 1)
                act.activation(sil[:, h, :], ps[:, 2 * h, :], ACT.Silu).then_inc(sil_done, 1)

            def u_hi_part(z, i, f, h):
                act.wait_ge(uf_done, 4 * ITERS * z + i * 4 + (2 * f + h + 1))
                act.activation(u_hi[:, f, half(h)], uf[:, h, :], ACT.Copy).then_inc(u_hi_done, 1)

            def ffn_step(z, i, last=False):
                w = W_FFN[z]
                after = 4 * ITERS * z + i * 4
                silu(z, i, 0, 0)
                u_hi_part(z, i, 0, 0)
                for k in (4, 5):
                    n = X_AT[z] + i * 16
                    free = (y_ready, n) if not isinstance(n, int) or n > 0 else None
                    hi_part(w, i, k, free)
                silu(z, i, 0, 1)
                u_hi_part(z, i, 0, 1)
                more = not (last and z == 1)
                for k in (0, 1) if more else ():
                    hi_part(w + CPI, i, k, (gu_ready, after + 2))
                silu(z, i, 1, 0)
                u_hi_part(z, i, 1, 0)
                silu(z, i, 1, 1)
                u_hi_part(z, i, 1, 1)
                for k in (2, 3) if more else ():
                    hi_part(w + CPI, i, k, (gu_ready, after + 4))

            def ffn(z):
                ffn_step(z, 0)
                with nc.scalar.Fori(1, ITERS - 1) as i:
                    ffn_step(z, i)
                ffn_step(z, ITERS - 1, last=True)
                tile = X_AT[z] + 16 * (ITERS - 1)
                norm(2 * z + 1, lambda h, c: (x_added, tile + KC * h + c + 1))

            def empty(p):
                what, m, h = TILES[p]
                if by_vector(p):
                    return
                if what == "in":
                    to = {KV: kvl[:, half(h)], Q0: ql[:, 0, half(h)], Q1: ql[:, 1, half(h)],
                          KA: k_a[:, half(h)], VA: vT[:, half(h)]}.get(m)
                    if to is None:
                        to = o_all[:, m - QA, half(h)]
                elif what == "knope":
                    to = k_nope[:, m, half(h)]
                else:
                    to = o_all[:, 4 + m, half(h)]
                act.wait_ge(tile_ready, p + 1)
                act.activation(to, ps[:, 4 + p % 4, :], ACT.Copy).then_inc(act_emptied, 1)

            def latent_square(v):
                source = (kvl[:, half(v)] if v < 2 else ql[:, v % 2, half((v - 2) // 2)])
                square(LAT_AT + v, source, (act_emptied, evacuated(2 * Q1 + 1)[1]))

            def latent_hi(v):
                to = kv_hi[:, half(v)] if v < 2 else q_hi[:, v % 2, half((v - 2) // 2)]
                if v == 0:
                    act.wait_ge(x_saved, 16)
                act.wait_ge(t_done, LAT_AT + v + 1)
                act.activation(to, tt[:, (LAT_AT + v) % 2, :], ACT.Copy).then_inc(n_hi, 1)

            def mixer_in():
                hi_of(W_IN + 4)
                for m in range(N_IN):
                    empty(2 * m)
                    hi_of(W_IN + m + 5)
                    empty(2 * m + 1)
                    if m == Q1:
                        latent_square(0)
                        latent_square(1)
                    if m == KA:
                        for v in range(2, 6):
                            latent_square(v)
                        for j, (tiles, bank, size) in enumerate(
                                [(1, 0, KV_RANK), (2, 2, KV_RANK), (4, 1, Q_RANK), (6, 3, Q_RANK)]):
                            deviation(LAT_STD_AT + j, LAT_AT + tiles, bank, size)
                    if VA <= m <= VA + 2:
                        latent_hi(2 * (m - VA))
                        latent_hi(2 * (m - VA) + 1)
                    if m == QA:
                        for j in range(2):
                            act.wait_ge(vt_ready, j + 1)
                            act.activation(v_a[:, 4 * j:4 * j + 4, :], ps[:, j, :].rearrange(
                                "p (b d) -> p b d", b=4), ACT.Copy).then_inc(va_done, 1)

            def exps(u):
                kind, a, i = UNITS[u]
                s = u % 2
                act.wait_ge(max_done, u + 1)
                if kind == "mla":
                    if u >= 2:
                        act.wait_ge(pt_ready, u - 1)
                    w = (i + 1) * P
                    act.activation(p_sb[:, s, 0:w], ps[:, 2 * s:2 * s + 2, :].rearrange("p b c -> p (b c)")[:, 0:w],
                                   ACT.Exp, bias=negm[:, s, 0:1], scale=MLA_SCALE,
                                   accum_out=den[:, s, 0:1]).then_inc(exp_done, 1)
                else:
                    w = P if i == 0 else 2 * P
                    for c in range(SWA_GROUP):
                        act.activation(p_sb[:, s, c * w:(c + 1) * w], p_sb[:, s, c * w:(c + 1) * w], ACT.Exp,
                                       bias=negm[:, s, c:c + 1], accum_out=den[:, s, c:c + 1])
                    act.activation(esink[:, s, :], dsink[:, s, :], ACT.Exp).then_inc(exp_done, 1)

            def copy_turned(u):
                act.wait_ge(pt_ready, u + 1)
                if u >= 2:
                    act.wait_ge(o_ready, u - 1)
                w = min(pt_cols(u), HALF)
                act.activation(pt_sb[:, u % 2, 0:w], ps[:, 4, 0:w], ACT.Copy).then_inc(pt_act, 1)

            def copy_output(u):
                kind, a, i = UNITS[u]
                act.wait_ge(o_ready, u + 1)
                if kind == "mla":
                    act.activation(o_all[:, 4 + a, blk(i)], ps[:, 6 + u % 2, 0:P], ACT.Copy).then_inc(o_done, 1)
                else:
                    g = SWA_DIM * a
                    act.activation(o_all[g:g + SWA_DIM, 0:SWA_GROUP, blk(i)],
                                   ps[g:g + SWA_DIM, 6 + u % 2, :].rearrange("p (c q) -> p c q", c=SWA_GROUP),
                                   ACT.Copy).then_inc(o_done, 1)

            def attention():
                for u in range(NU + 2):
                    if u < NU:
                        exps(u)
                    if 1 <= u <= NU:
                        copy_turned(u - 1)
                    if u >= 2:
                        copy_output(u - 2)

            def mixer_out():
                act.wait_ge(o_done, NU)
                for h in range(NH2):
                    for c in range(KC):
                        act.activation(h_hi[:, c, half(h)], o_all[:, c, half(h)], ACT.Copy).then_inc(o_hi, 1)
                for d in range(1, 7):
                    hi_of(W_OUT + d + 5)

            act.dma_start(c_act[:], c_in).then_inc(c_landed, 16)
            act.dma_start(small[:], small_in).then_inc(small_landed, 16)
            act.dma_start(consts[:], const_in).then_inc(const_landed, 16)
            act.dma_start(sinks[:], sinks_in).then_inc(sinks_landed, 16)
            act.wait_ge(c_landed, 16)
            act.activation(c_act[:], c_act[:], ACT.Silu).then_inc(c_ready, 1)
            act.wait_ge(eps_ready, 1)
            for k in range(4):
                hi_part(k, 0, 0, None)
            first_norm()
            ffn(0)
            mixer_in()
            for p in range(MLA_FIRST, len(TILES)):
                empty(p)
            for n in range(W_OUT + 2, W_OUT + 6):
                hi_of(n)
            attention()
            mixer_out()
            norm(2, lambda h, c: (x_added, X_MIX + 2 * c + h + 1))
            ffn(1)

        @block.vector
        def _(dve):
            count = {}

            def step(ins, signal):
                count[signal.name] = count.get(signal.name, 0) + 1
                ins.then_inc(signal, 1)
                dve.wait_ge(signal, count[signal.name])

            def modulation(j):
                for k in range(4):
                    dve.wait_ge(mod_landed[k], j * 16 + 16)
                    if not isinstance(j, int) or j > 0:
                        dve.wait_ge(mod_ready, j)
                    dve.tensor_tensor_reduce(out=mod_raw[:, k, :], in0=mod_raw[:, k, :], in1=c_act[:],
                                             scale=1.0, scalar=0.0, op0=ALU.mult, op1=ALU.add,
                                             accum_out=mod_acc[:, k:k + 1]).then_inc(mod_used, 1)
                dve.wait_ge(mod_used, j * 4 + 4)
                dve.tensor_tensor(mod[:, bass.ds(j * 4, 4)], mod_acc[:], small[:, bass.ds(j * 4, 4)],
                                  ALU.add).then_inc(mod_ready, 1)

            def scale_vector(s):
                dve.wait_ge(mod_ready, 6 * s + 4)
                c0 = 3 * KC * s + KC
                dve.scalar_tensor_tensor(out=scale_v[:, s, :], in0=mod[:, c0:c0 + KC], scalar=1.0,
                                         in1=gain(s), op0=ALU.add, op1=ALU.mult).then_inc(vec_ready, 1)

            def gate_vector(s):
                dve.wait_ge(mod_ready, 6 * s + 6)
                c0 = 3 * KC * s + 2 * KC
                dve.tensor_scalar(gate_v[:, s, :], mod[:, c0:c0 + KC], 1.0 if s == 1 else 0.5, None,
                                  ALU.mult).then_inc(vec_ready, 1)

            def lo_part(base, i, k):
                dve.wait_ge(hi_split, i * CPI + (base + k + 1))
                s = (base + k) % SPLIT
                dve.tensor_tensor(w_lo[:, s, :], w_raw[:, (base + k) % RAW, :], w_hi[:, s, :].bitcast(F32),
                                  ALU.subtract).then_inc(lo_split, 1)

            def lo_of(n):
                lo_part(n, 0, 0)

            def invert(n):
                dve.wait_ge(std_done, n + 1)
                dve.reciprocal(rstd[:, n % 2, :], std[:, n % 2, :]).then_inc(rstd_done, 1)

            def scaled(n, source, scale, r):
                dve.wait_ge(rstd_done, r + 1)
                if n >= 2:
                    dve.wait_ge(n_lo, n - 1)
                dve.scalar_tensor_tensor(out=tt[:, n % 2, :], in0=source, scalar=scale, in1=rstd[:, r % 2, :],
                                         op0=ALU.mult, op1=ALU.mult).then_inc(t_done, 1)

            def shifted_lo(s, h, c):
                n = NORM_AT[s] + KC * h + c
                dve.wait_ge(n_hi, n + 1)
                dve.scalar_tensor_tensor(out=h_lo[:, c, half(h)], in0=tt[:, n % 2, :],
                                         scalar=mod[:, 3 * KC * s + c:3 * KC * s + c + 1],
                                         in1=h_hi[:, c, half(h)].bitcast(F32), op0=ALU.add,
                                         op1=ALU.subtract).then_inc(n_lo, 1)

            def norm_half(s, h, between=lambda c: None):
                invert(STD_AT[s] + h)
                for c in range(KC + 1):
                    if c < KC:
                        scaled(NORM_AT[s] + KC * h + c, x[:, c, half(h)], scale_v[:, s, c:c + 1], STD_AT[s] + h)
                    if c >= 1:
                        shifted_lo(s, h, c - 1)
                    between(c)

            def final_half(h, between=lambda c: None):
                invert(STD_AT[3] + h)
                dve.wait_ge(rstd_done, STD_AT[3] + h + 1)
                for c in range(KC):
                    dve.scalar_tensor_tensor(out=x[:, c, half(h)], in0=x[:, c, half(h)],
                                             scalar=gain(3)[:, c:c + 1], in1=rstd[:, h, :],
                                             op0=ALU.mult, op1=ALU.mult).then_inc(out_ready, 1)
                    between(c)

            def multiply(z, i, f, h):
                n = 4 * ITERS * z + i * 4 + (2 * f + h)
                dve.wait_ge(sil_done, n + 1)
                if not isinstance(n, int) or n >= 2:
                    dve.wait_ge(u_lo_done, n - 1)
                dve.tensor_tensor(uf[:, h, :], sil[:, h, :], ps[:, 2 * h + 1, :], ALU.mult).then_inc(uf_done, 1)
                dve.wait_ge(u_hi_done, n + 1)
                dve.tensor_tensor(u_lo[:, f, half(h)], uf[:, h, :], u_hi[:, f, half(h)].bitcast(F32),
                                  ALU.subtract).then_inc(u_lo_done, 1)

            def add(n, bank, d, h, s):
                dve.wait_ge(y_ready, n + 1)
                dve.scalar_tensor_tensor(out=x[:, d, half(h)], in0=ps[:, bank, :], scalar=gate_v[:, s, d:d + 1],
                                         in1=x[:, d, half(h)], op0=ALU.mult, op1=ALU.add).then_inc(x_added, 1)

            def ffn_step(z, i, first=False, last=False):
                w = W_FFN[z]
                more = not (last and z == 1)
                multiply(z, i, 0, 0)
                if z == 0 and first:
                    modulation(4)
                for k in (4, 5):
                    lo_part(w, i, k)
                multiply(z, i, 0, 1)
                if z == 0 and first:
                    modulation(5)
                    gate_vector(0)
                    dve.wait_ge(vec_ready, 2)
                for k in (0, 1) if more else ():
                    lo_part(w + CPI, i, k)
                multiply(z, i, 1, 0)
                if z == 0 and first:
                    modulation(6)
                multiply(z, i, 1, 1)
                for k in (2, 3) if more else ():
                    lo_part(w + CPI, i, k)
                if z == 0:
                    modulation(i + 7)

                def added(h, d):
                    add(X_AT[z] + i * 16 + (KC * h + d), 4 + d % 4, d, h, 2 * z)

                for d in range(KC):
                    added(0, d)
                if not last:
                    for d in range(KC):
                        added(1, d)
                    return
                if z == 0:
                    for s in (1, 2):
                        scale_vector(s)
                        gate_vector(s)
                    dve.wait_ge(vec_ready, 6)
                for d in range(4):
                    added(1, d)

                def between(c):
                    if 4 + c < KC:
                        added(1, 4 + c)

                if z == 0:
                    norm_half(1, 0, between)
                    norm_half(1, 1)
                else:
                    final_half(0, between)
                    final_half(1)

            def ffn(z):
                ffn_step(z, 0, first=True)
                with nc.vector.Fori(1, ITERS - 1) as i:
                    ffn_step(z, i)
                ffn_step(z, ITERS - 1, last=True)

            def rotate_key(h):
                p = 2 * KROPE + h
                bank = ps[:, 4 + p % 4, :]
                if h == 0:
                    dve.wait_ge(tab_landed, 16)
                dve.wait_ge(tile_ready, p + 1)
                r = slice(0, ROPE)
                dve.tensor_tensor(tt[r, 0, :], bank[r, :], tab[r, 0, half(h)], ALU.mult)
                step(dve.tensor_tensor(tt[r, 1, :], bank[ROPE:P, :], tab[ROPE:P, 1, half(h)], ALU.mult),
                     rope_part)
                dve.tensor_tensor(k_r[r, half(h)], tt[r, 0, :], tt[r, 1, :], ALU.add)
                dve.tensor_tensor(k_r[ROPE:P, half(h)], tt[r, 0, :], tt[r, 1, :], ALU.add
                                  ).then_inc(dve_emptied, 1)
                dve.wait_ge(dve_emptied, h + 1)

            def rotate_query(p):
                _, r, h = TILES[p]
                dve.wait_ge(tile_ready, p + 2)
                dve.tensor_tensor(tt[:, 0, :], ps[:, 4 + p % 4, :], tab[:, 0, half(h)], ALU.mult
                                  ).then_inc(dve_emptied, 1)
                dve.tensor_tensor(tt[:, 1, :], ps[:, 4 + (p + 1) % 4, :], tab[:, 1, half(h)], ALU.mult
                                  ).then_inc(dve_emptied, 1)
                dve.wait_ge(dve_emptied, evacuated(p + 1)[1])
                step(dve.tensor_tensor(q_r[:, r, half(h)], tt[:, 0, :], tt[:, 1, :], ALU.add), rope_done)

            def latent(v):
                h = v if v < 2 else (v - 2) // 2
                source = kvl[:, half(h)] if v < 2 else ql[:, v % 2, half(h)]
                g = lat_gain[:, 2:3] if v < 2 else lat_gain[:, v % 2:v % 2 + 1]
                r = LAT_STD_AT + (h if v < 2 else 2 + h)
                if v in (0, 1, 2, 4):
                    invert(r)
                scaled(LAT_AT + v, source, g, r)

            def latent_lo(v):
                h = v if v < 2 else (v - 2) // 2
                hi, lo = (kv_hi[:, half(h)], kv_lo[:, half(h)]) if v < 2 else (
                    q_hi[:, v % 2, half(h)], q_lo[:, v % 2, half(h)])
                dve.wait_ge(n_hi, LAT_AT + v + 1)
                dve.tensor_tensor(lo, tt[:, (LAT_AT + v) % 2, :], hi.bitcast(F32), ALU.subtract
                                  ).then_inc(n_lo, 1)

            def mixer_in():
                lo_of(W_IN + 4)
                for m in range(N_IN):
                    lo_of(W_IN + m + 5)
                    if m == KROPE:
                        rotate_key(0)
                        rotate_key(1)
                    if KA <= m <= KA + 3:
                        v = 2 * (m - KA)
                        for w in (v - 2, v - 1) if v else ():
                            latent_lo(w)
                        for w in (v, v + 1) if v < 6 else ():
                            latent(w)

            def empty_value(p):
                dve.wait_ge(tile_ready, p + 1)
                dve.tensor_copy(v_b[:, TILES[p][2], :], ps[:, 4 + p % 4, :]).then_inc(dve_emptied, 1)

            def latent_products():
                for p in range(MLA_FIRST, len(TILES)):
                    if TILES[p][0] == "v":
                        empty_value(p)
                    if TILES[p][0] == "rope":
                        rotate_query(p)
                for n in range(W_OUT + 2, W_OUT + 6):
                    lo_of(n)
                dve.wait_ge(line_ready, 1)
                dve.wait_ge(lm_landed, 16)
                dve.tensor_tensor(line[:], ps[0:SWA_HEADS, 2, 0:LINE], linemask[:], ALU.add
                                  ).then_inc(line_added, 1)

            def maxima(u):
                kind, a, i = UNITS[u]
                s = u % 2
                dve.wait_ge(s_ready, u + 1)
                scores = ps[:, 2 * s:2 * s + 2, :].rearrange("p b c -> p (b c)")
                if kind == "mla":
                    step(dve.tensor_reduce(mx[:, s, 0:1], scores[:, 0:(i + 1) * P], AX.X, ALU.max), max_part)
                    dve.tensor_scalar(negm[:, s, 0:1], mx[:, s, 0:1], -MLA_SCALE, None, ALU.mult
                                      ).then_inc(max_done, 1)
                    return
                w = P if i == 0 else 2 * P
                if u >= 2:
                    dve.wait_ge(pt_ready, u - 1)
                heads = slice(SWA_GROUP * a, SWA_GROUP * a + SWA_GROUP)
                p4 = p_sb[:, s, 0:SWA_GROUP * w].rearrange("p (c k) -> p c k", c=SWA_GROUP)
                step(dve.scalar_tensor_tensor(
                    out=p4, in0=scores[:, 0:SWA_GROUP * w].rearrange("p (c k) -> p c k", c=SWA_GROUP),
                    scalar=SWA_SCALE, in1=bias[:, heads, 2 * P - w:2 * P], op0=ALU.mult, op1=ALU.add), biased)
                step(dve.tensor_reduce(mx[:, s, :], p4, AX.X, ALU.max), max_part)
                step(dve.tensor_tensor(mx[:, s, :], mx[:, s, :], sinks[:, heads], ALU.max), max_part)
                dve.tensor_scalar(negm[:, s, :], mx[:, s, :], -1.0, None, ALU.mult)
                dve.tensor_tensor(dsink[:, s, :], sinks[:, heads], mx[:, s, :], ALU.subtract
                                  ).then_inc(max_done, 1)

            def normalise(u):
                kind, a, i = UNITS[u]
                s = u % 2
                dve.wait_ge(exp_done, u + 1)
                if kind == "mla":
                    w = (i + 1) * P
                    step(dve.reciprocal(rden[:, s, 0:1], den[:, s, 0:1]), den_part)
                    dve.tensor_scalar(p_sb[:, s, 0:w], p_sb[:, s, 0:w], rden[:, s, 0:1], None, ALU.mult
                                      ).then_inc(p_done, 1)
                    return
                w = P if i == 0 else 2 * P
                step(dve.tensor_tensor(den[:, s, :], den[:, s, :], esink[:, s, :], ALU.add), den_part)
                step(dve.reciprocal(rden[:, s, :], den[:, s, :]), den_part)
                for c in range(SWA_GROUP):
                    ins = dve.tensor_scalar(p_sb[:, s, c * w:(c + 1) * w], p_sb[:, s, c * w:(c + 1) * w],
                                            rden[:, s, c:c + 1], None, ALU.mult)
                ins.then_inc(p_done, 1)

            def copy_turned(u):
                w = pt_cols(u) - HALF
                if w <= 0:
                    return
                dve.wait_ge(pt_ready, u + 1)
                if u >= 2:
                    dve.wait_ge(o_ready, u - 1)
                dve.tensor_copy(pt_sb[:, u % 2, HALF:HALF + w], ps[:, 5, 0:w]).then_inc(pt_dve, 1)

            def attention():
                dve.wait_ge(sinks_landed, 16)
                dve.wait_ge(bias_landed, 16)
                for u in range(NU + 1):
                    if u >= 1:
                        normalise(u - 1)
                    if u < NU:
                        maxima(u)
                    if u >= 1:
                        copy_turned(u - 1)

            def mixer_out():
                for h in range(NH2):
                    for c in range(KC):
                        dve.wait_ge(o_hi, KC * h + c + 1)
                        dve.tensor_tensor(h_lo[:, c, half(h)], o_all[:, c, half(h)],
                                          h_hi[:, c, half(h)].bitcast(F32), ALU.subtract).then_inc(o_lo, 1)
                dve.wait_ge(x_back, 16)
                for d in range(KC):
                    for h in range(NH2):
                        w = 2 * d + h
                        add(X_MIX + w, 4 + w % 4, d, h, 1)
                    if 1 <= d <= 6:
                        lo_of(W_OUT + d + 5)

            dve.memset(eps[:], EPS).then_inc(eps_ready, 1)
            dve.wait_ge(small_landed, 16)
            dve.wait_ge(c_ready, 1)
            for j in range(2):
                modulation(j)
            for k in range(4):
                lo_part(k, 0, 0)
            for j in range(2, 4):
                modulation(j)
            scale_vector(0)
            dve.wait_ge(vec_ready, 1)
            norm_half(0, 0)
            norm_half(0, 1)
            ffn(0)
            mixer_in()
            latent_products()
            attention()
            mixer_out()
            norm_half(2, 0)
            norm_half(2, 1)
            ffn(1)


def _columns(w, cols):
    return w[:, cols].reshape(-1, P, P).transpose(1, 0, 2).reshape(P, -1)


def weight_stream(np, gate1, up1, down1, w_in, w_uq, w_ukv, w_o, gate2, up2, down2):
    chunks = []

    def ffn(gate, up, down):
        for i in range(ITERS):
            fs = [slice((FPI * i + f) * P, (FPI * i + f + 1) * P) for f in range(FPI)]
            for f in fs:
                chunks.append(_columns(gate, f))
                chunks.append(_columns(up, f))
            for f in fs:
                chunks.append(down[f, :])

    ffn(gate1, up1, down1)
    r = np.arange
    q_at, k_at, v_at, ql_at, kv_at, kr_at = 0, 512, 640, 768, 1024, 1152
    rope = r(kr_at, kr_at + ROPE)
    swapped = np.concatenate([rope[ROPE // 2:], rope[:ROPE // 2]])
    for cols in ([r(kv_at, kv_at + P), r(ql_at, ql_at + P), r(ql_at + P, ql_at + 2 * P),
                  np.concatenate([rope, swapped]), r(k_at, k_at + P), r(v_at, v_at + P)]
                 + [np.concatenate([r(q_at + 64 * c, q_at + 64 * c + 64),
                                    r(q_at + 256 + 64 * c, q_at + 256 + 64 * c + 64)]) for c in range(4)]):
        chunks.append(_columns(w_in, cols))
    hd = NOPE + ROPE
    nope = np.concatenate([r(h * hd, h * hd + NOPE) for h in range(MLA_HEADS)])
    rope = [r(h * hd + NOPE, (h + 1) * hd) for h in range(MLA_HEADS)]
    swapped = [np.concatenate([c[ROPE // 2:], c[:ROPE // 2]]) for c in rope]
    cols = np.concatenate([nope, *rope, *swapped])
    for k in range(2):
        chunks.append(w_uq[k * P:(k + 1) * P, cols])
    chunks.append(w_ukv[:, np.concatenate([r(h * 256 + o, h * 256 + o + P) for o in (0, P)
                                           for h in range(MLA_HEADS)])])
    rows = np.concatenate([np.concatenate([r(64 * c, 64 * c + 64), r(256 + 64 * c, 256 + 64 * c + 64)])
                           for c in range(4)] + [r(512, 1024)])
    for d in range(KC):
        chunks.append(_columns(w_o[rows, :], slice(d * P, (d + 1) * P)))
    ffn(gate2, up2, down2)
    return np.stack(chunks)


def shape_constants(np):
    f = np.float32
    causal = np.where(np.arange(P)[None, :] > np.arange(P)[:, None], f(-1e30), f(0))
    consts = np.stack([np.eye(P, dtype=f), causal.astype(f), np.ones((P, P), f)], axis=1)
    inv = np.power(f(10000.0), -np.arange(0, ROPE, 2, dtype=f) / f(ROPE)).astype(f)
    ang = (np.arange(T, dtype=f)[:, None] * inv[None, :]).astype(f)
    cos, sin = np.cos(ang).T.astype(f), np.sin(ang).T.astype(f)
    tab = np.stack([np.concatenate([cos, cos, cos, cos]), np.concatenate([-sin, sin, -sin, sin])], axis=1)
    dist = 2 * P - 1 - np.arange(LINE)
    ok = (dist >= 0) & (dist < P)
    n = np.maximum(dist, 0)
    large = 16 + (np.log(np.maximum(n, 1).astype(f) / f(16)) / f(np.log(8.0)) * f(16)).astype(np.int32)
    bucket = np.where(n < 16, n, np.minimum(large, BUCKETS - 1))
    onehot = ((bucket[None, :] == np.arange(BUCKETS)[:, None]) & ok[None, :]).astype(f)
    linemask = np.broadcast_to(np.where(ok, f(0), f(-1e30)), (SWA_HEADS, LINE)).astype(f)
    return consts, tab, onehot, linemask


def kernel(x, c, w_mod, b_mod, norm_ffn1, ffn1_gate, ffn1_up, ffn1_down, norm_mix, w_in, q_norm, kv_norm,
           w_uq, w_ukv, sinks, w_o, norm_ffn2, ffn2_gate, ffn2_up, ffn2_down, rel_bias, norm_final):
    import numpy as np
    import concourse.bacc as bacc
    from concourse.bass_utils import run_bass_kernel_spmd

    def a(v):
        return np.asarray(v)

    def by_partition(v):
        return a(v).reshape(-1, P).T

    consts, tab, onehot, linemask = shape_constants(np)
    arrays = {
        "xT_in": a(x)[0].T.reshape(KC, P, T).transpose(1, 0, 2),
        "c_in": np.broadcast_to(a(c)[0], (P, D)),
        "w_modT_in": a(w_mod)[0].T.reshape(MODC, P, D),
        "small_in": np.concatenate([by_partition(v) for v in (
            a(b_mod)[0], a(norm_ffn1)[0], a(norm_mix)[0], a(norm_ffn2)[0], a(norm_final), a(q_norm)[0],
            a(kv_norm)[0])], axis=1),
        "wstream_in": weight_stream(np, *(a(w)[0] for w in (
            ffn1_gate, ffn1_up, ffn1_down, w_in, w_uq, w_ukv, w_o, ffn2_gate, ffn2_up, ffn2_down))),
        "const_in": consts,
        "tab_in": tab,
        "sinks_in": np.broadcast_to(a(sinks)[0], (P, SWA_HEADS)),
        "rel_in": a(rel_bias),
        "oh_in": onehot,
        "lm_in": linemask,
    }
    arrays = {n: np.ascontiguousarray(v) for n, v in arrays.items()}
    nc = bacc.Bacc("TRN2", target_bir_lowering=False, num_devices=1, dynamic_dma_scratch_size=4096)
    args = [nc.dram_tensor(n, v.shape, F32, kind="ExternalInput").ap() for n, v in arrays.items()]
    out = nc.dram_tensor("out", (P, KC, T), F32, kind="ExternalOutput").ap()
    build(nc, *args, out)
    r = run_bass_kernel_spmd(nc, [arrays], core_ids=[0])
    got = r.results[0]["out"]
    return got.transpose(1, 0, 2).reshape(D, T).T.reshape(1, T, D)
```

```python
from contextlib import ExitStack

import concourse.bass as bass
from concourse import mybir
from concourse.alu_op_type import AluOpType as ALU

F32 = mybir.dt.float32
F32R = mybir.dt.float32r
ACT = mybir.ActivationFunctionType
AX = mybir.AxisListType

P = 128
D = 1024
T = 1024
KC = D // P
HALF = 512
NH2 = T // HALF
D_FF = 2816
FPI = 2
ITERS = D_FF // P // FPI
N_MOD = 9
MODC = N_MOD * KC
EPS = 1e-6

SWA_HEADS = 8
SWA_GROUP = 4
SWA_DIM = 64
MLA_HEADS = 4
NOPE = 128
ROPE = 64
Q_RANK = 256
KV_RANK = 128
NBLK = T // P
BUCKETS = 32
LINE = 384
MLA_SCALE = (NOPE + ROPE) ** -0.5
SWA_SCALE = SWA_DIM ** -0.5

CPI = 3 * FPI
W_FFN = [0, CPI * ITERS + 21]
W_IN = CPI * ITERS
N_IN = 10
W_UQ = W_IN + N_IN
W_UKV = W_UQ + 2
W_OUT = W_UKV + 1
N_CHUNKS = 2 * CPI * ITERS + 21
RAW, SPLIT = 3, 6
P_SLOTS = 3

NORM_AT = [0, 16, 38, 54]
LAT_AT = 32
STD_AT = [0, 2, 8, 10]
LAT_STD_AT = 4
X_AT = [0, 16 * ITERS + 16]
X_MIX = 16 * ITERS
MLA_FIRST = 2 * N_IN
SMALL = MODC + 4 * KC + 3


def units():
    mla = [("mla", h, i) for i in range(NBLK) for h in range(MLA_HEADS)]
    swa = [("swa", g, i) for i in range(NBLK) for g in range(2)]
    out = []
    for n in range(16):
        out += [mla[n], swa[n], mla[31 - n]]
    return out


def mixer_tiles():
    out = []
    for m in range(N_IN):
        out += [("in", m, h) for h in range(NH2)]
    out += [("knope", hd, h) for hd in range(MLA_HEADS) for h in range(NH2)]
    out += [("v", 0, b) for b in range(NBLK)]
    out += [("qnope", hd, h) for hd in range(MLA_HEADS) for h in range(NH2)]
    for r in range(2):
        for h in range(NH2):
            out += [("rope", r, h), ("swapped", r, h)]
    return out


KV, Q0, Q1, KROPE, KA, VA, QA = 0, 1, 2, 3, 4, 5, 6
TILES = mixer_tiles()


def by_vector(p):
    what, m, _ = TILES[p]
    return what in ("v", "rope", "swapped") or (what == "in" and m == KROPE)


def evacuated(p):
    mine = by_vector(p)
    return mine, sum(by_vector(q) == mine for q in range(p + 1))


def build(nc, xT, c_in, w_modT, small_in, wstream, const_in, tab_in, sinks_in, rel_in, oh_in, lm_in,
          out):
    ctx = ExitStack()
    with ctx:
        at = [4224]

        def sb(name, shape, dt, offset=None):
            size = 4
            for s in shape[1:]:
                size *= s
            if offset is None:
                offset = at[0]
                at[0] += (size + 31) // 32 * 32
            return nc.alloc_sbuf_tensor_at(name, shape, dt, offset=offset)

        x = sb("x", [P, KC, T], F32)
        h_at = at[0]
        h_hi = sb("h_hi", [P, KC, T], F32R)
        h_lo = sb("h_lo", [P, KC, T], F32R)
        w_raw = sb("w_raw", [P, RAW, D], F32)
        w_hi = sb("w_hi", [P, SPLIT, D], F32R)
        w_lo = sb("w_lo", [P, SPLIT, D], F32R)
        s_at = at[0]
        u_hi = sb("u_hi", [P, FPI, T], F32R)
        u_lo = sb("u_lo", [P, FPI, T], F32R)
        sil = sb("sil", [P, NH2, HALF], F32)
        uf = sb("uf", [P, NH2, HALF], F32)
        mod_raw = sb("mod_raw", [P, 4, D], F32)
        c_act = sb("c_act", [P, D], F32)
        tt = sb("tt", [P, 2, HALF], F32)
        p_at = at[0]
        sq = sb("sq", [P, 2, HALF], F32)
        diag = sb("diag", [P, 2, HALF], F32)
        acc = sb("acc", [P, 2, HALF], F32)
        small = sb("small", [P, SMALL], F32)
        consts = sb("consts", [P, 3, P], F32)
        mod = sb("mod", [P, MODC], F32)
        mod_acc = sb("mod_acc", [P, 4], F32)
        scale_v = sb("scale_v", [P, 3, KC], F32)
        gate_v = sb("gate_v", [P, 3, KC], F32)
        sinks = sb("sinks", [P, SWA_HEADS], F32)
        mx = sb("mx", [P, 2, 4], F32)
        negm = sb("negm", [P, 2, 4], F32)
        dsink = sb("dsink", [P, 2, 4], F32)
        esink = sb("esink", [P, 2, 4], F32)
        den = sb("den", [P, 2, 4], F32)
        rden = sb("rden", [P, 2, 4], F32)
        eps = sb("eps", [P, 1], F32)
        std = sb("std", [P, 4, 4], F32)
        rstd = sb("rstd", [P, 4, 4], F32)
        o_all = sb("o_all", [P, KC, T], F32, s_at)
        kvl = sb("kvl", [P, T], F32, s_at + 16384)
        ql = sb("ql", [P, 2, T], F32, s_at + 20480)
        vT = sb("vT", [P, T], F32, s_at + 28672)
        k_a = sb("k_a", [P, T], F32, s_at + 32768)
        v_a = sb("v_a", [P, NBLK, P], F32, s_at + 36864)
        k_r = sb("k_r", [P, T], F32, s_at + 40960)
        x_at = h_at - 32768
        q_hi = sb("q_hi", [P, 2, T], F32R, x_at)
        q_lo = sb("q_lo", [P, 2, T], F32R, x_at + 8192)
        kv_hi = sb("kv_hi", [P, T], F32R, x_at + 16384)
        kv_lo = sb("kv_lo", [P, T], F32R, x_at + 20480)
        tab = sb("tab", [P, 2, T], F32, x_at + 24576)
        k_nope = sb("k_nope", [P, MLA_HEADS, T], F32, h_at)
        v_b = sb("v_b", [P, NBLK, MLA_HEADS * P], F32, h_at + 16384)
        q_r = sb("q_r", [P, 2, T], F32, h_at + 32768)
        pt_sb = sb("pt_sb", [P, 2, D], F32, h_at + 40960)
        bias = sb("bias", [P, SWA_HEADS, 2 * P], F32, h_at + 49152)
        p_sb = sb("p_sb", [P, P_SLOTS, D], F32, p_at)
        onehot = sb("onehot", [BUCKETS, LINE], F32, s_at)
        linemask = sb("linemask", [SWA_HEADS, LINE], F32, s_at + 1536)
        line = sb("line", [SWA_HEADS, LINE], F32, s_at + 3072)
        rel = sb("rel", [BUCKETS, SWA_HEADS], F32, s_at + 4608)

        ident, mask, ones = (consts[:, j, :] for j in range(3))
        bmod = small[:, 0:MODC]

        def gain(s):
            return small[:, MODC + KC * s:MODC + KC * s + KC]

        lat_gain = small[:, MODC + 4 * KC:SMALL]

        ps = ctx.enter_context(nc.psum_tensor("ps", [P, 8, HALF], F32))

        x_save = nc.dram_tensor("x_save", [P, KC, T], F32).ap()
        line_dram = nc.dram_tensor("line_dram", [P, SWA_HEADS, LINE], F32)

        def sem(name):
            return ctx.enter_context(nc.semaphore(name))

        x_landed = [sem(f"x_landed{j}") for j in range(2)]
        c_landed = sem("c_landed")
        small_landed = sem("small_landed")
        const_landed = sem("const_landed")
        eps_ready = sem("eps_ready")
        sinks_landed = sem("sinks_landed")
        sum_used = sem("sum_used")
        raw_landed = [sem(f"raw_landed{j}") for j in range(RAW)]
        hi_split = sem("hi_split")
        lo_split = sem("lo_split")
        mod_landed = [sem(f"mod_landed{j}") for j in range(4)]
        mod_used = sem("mod_used")
        mod_ready = sem("mod_ready")
        vec_ready = sem("vec_ready")
        c_ready = sem("c_ready")
        sq_done = sem("sq_done")
        stat_done = sem("stat_done")
        std_done = sem("std_done")
        rstd_done = sem("rstd_done")
        diag_done = sem("diag_done")
        r_ready = sem("r_ready")
        summed = sem("summed")
        t_done = sem("t_done")
        n_hi = sem("n_hi")
        n_lo = sem("n_lo")
        gu_ready = sem("gu_ready")
        sil_done = sem("sil_done")
        uf_done = sem("uf_done")
        u_hi_done = sem("u_hi_done")
        u_lo_done = sem("u_lo_done")
        y_ready = sem("y_ready")
        x_added = sem("x_added")
        x_saved = sem("x_saved")
        tab_landed = sem("tab_landed")
        oh_landed = sem("oh_landed")
        rel_landed = sem("rel_landed")
        lm_landed = sem("lm_landed")
        line_ready = sem("line_ready")
        line_added = sem("line_added")
        line_saved = sem("line_saved")
        bias_landed = sem("bias_landed")
        x_back = sem("x_back")
        tile_ready = sem("tile_ready")
        act_emptied = sem("act_emptied")
        dve_emptied = sem("dve_emptied")
        rope_part = sem("rope_part")
        rope_done = sem("rope_done")
        vt_ready = sem("vt_ready")
        va_done = sem("va_done")
        s_ready = sem("s_ready")
        biased = sem("biased")
        max_part = sem("max_part")
        max_done = sem("max_done")
        exp_done = sem("exp_done")
        den_part = sem("den_part")
        p_done = sem("p_done")
        pt_ready = sem("pt_ready")
        pt_act = sem("pt_act")
        pt_dve = sem("pt_dve")
        o_ready = sem("o_ready")
        o_done = sem("o_done")
        o_hi = sem("o_hi")
        o_lo = sem("o_lo")
        out_ready = sem("out_ready")
        out_saved = sem("out_saved")

        def half(h):
            return slice(h * HALF, (h + 1) * HALF)

        def blk(i):
            return slice(i * P, (i + 1) * P)

        def slots(n):
            return n % RAW, n % SPLIT

        N_ACT = sum(not by_vector(p) for p in range(len(TILES)))
        N_DVE = len(TILES) - N_ACT
        UNITS = units()
        NU = len(UNITS)

        def r_bank(n):
            return (0, 2, 1, 3)[n - LAT_STD_AT] if 0 <= n - LAT_STD_AT < 4 else 2 + n % 2

        def pt_cols(u):
            kind, _, i = UNITS[u]
            return (i + 1) * P if kind == "mla" else SWA_GROUP * (P if i == 0 else 2 * P)

        block = ctx.enter_context(nc.Block())

        @block.sync
        def _(sp):
            for h in range(NH2):
                sp.dma_start(x[:, :, half(h)], xT[:, :, half(h)]).then_inc(x_landed[h], 16)
            sp.wait_ge(mod_used, 2 * KC - 4)
            for n in range(RAW):
                sp.dma_start(w_raw[:, n, :], wstream[n]).then_inc(raw_landed[n], 16)
            with nc.sync.Fori(1, N_CHUNKS // RAW) as g:
                for j in range(RAW):
                    sp.wait_ge(lo_split, g * RAW + (j - RAW + 1))
                    sp.dma_start(w_raw[:, j, :], wstream[bass.ds(g * RAW + j, 1), :, :].rearrange(
                        "a p d -> (a p) d")).then_inc(raw_landed[j], 16)
            for h in range(NH2):
                for c in range(0, KC, 2):
                    sp.wait_ge(out_ready, KC * h + c + 2)
                    sp.dma_start(out[:, c:c + 2, half(h)], x[:, c:c + 2, half(h)]).then_inc(out_saved, 16)
            sp.wait_ge(out_saved, 16 * KC)

        @block.gpsimd
        def _(pool):
            def sum_squares(s):
                for h in range(NH2):
                    for c in range(1, KC):
                        n = NORM_AT[s] + KC * h + c
                        pool.wait_ge(sq_done, n + 1)
                        done = (KC - 1) * (NH2 * (s - 1) + h) + c - 1
                        if c == 1 and s > 1:
                            pool.wait_ge(sum_used, NH2 * (s - 2) + h + 1)
                        if c > 1:
                            pool.wait_ge(summed, done)
                        first = acc[:, h, :] if c > 1 else sq[:, (n - 1) % 2, :]
                        nc.gpsimd.tensor_tensor(acc[:, h, :], first, sq[:, n % 2, :], ALU.add
                                                ).then_inc(summed, 1)

            for j in range(4):
                pool.dma_start(mod_raw[:, j, :], w_modT[j]).then_inc(mod_landed[j], 16)
            with nc.gpsimd.Fori(1, MODC // 4) as g:
                for j in range(4):
                    pool.wait_ge(mod_used, g * 4 + (j - 3))
                    pool.dma_start(mod_raw[:, j, :], w_modT[bass.ds(g * 4 + j, 1), :, :].rearrange(
                        "a p d -> (a p) d")).then_inc(mod_landed[j], 16)
            sum_squares(1)
            pool.dma_start(x_save, x[:]).then_inc(x_saved, 16)
            pool.wait_ge(x_saved, 16)
            pool.wait_ge(n_lo, LAT_AT)
            pool.dma_start(tab[:], tab_in).then_inc(tab_landed, 16)
            pool.wait_ge(tile_ready, 2 * N_IN)
            pool.wait_ge(line_saved, 16)
            pool.dma_start(bias[:], bass.AP(line_dram, P - 1, [[SWA_HEADS * LINE - 1, P], [LINE, SWA_HEADS],
                                                               [1, 2 * P]])).then_inc(bias_landed, 16)
            pool.wait_ge(tile_ready, len(TILES))
            pool.wait_ge(rope_done, 4)
            pool.dma_start(x[:], x_save).then_inc(x_back, 16)
            pool.wait_ge(x_back, 16)
            sum_squares(2)
            sum_squares(3)

        @block.tensor
        def _(pe):
            def product(psum, wh, wl, ah, al, start, stop):
                pe.matmul(psum, wh, al, start=start, stop=False)
                pe.matmul(psum, wl, ah, start=False, stop=False)
                return pe.matmul(psum, wh, ah, start=False, stop=stop)

            def stats(first, tiles, bank):
                for k in range(tiles):
                    pe.wait_ge(sq_done, first + k + 1)
                    for b in range(HALF // P):
                        mm = pe.matmul(ps[:, bank, b:b + 1], sq[:, (first + k) % 2, blk(b)], ones[:, 0:1],
                                       start=(k == 0 and b == 0), stop=(k == tiles - 1),
                                       skip_group_check=True)
                    mm.then_inc(stat_done, 1)

            def total(s, h):
                pe.wait_ge(summed, (KC - 1) * (NH2 * (s - 1) + h + 1))
                for b in range(HALF // P):
                    mm = pe.matmul(ps[:, r_bank(STD_AT[s] + h), b:b + 1], acc[:, h, blk(b)], ones[:, 0:1],
                                   start=(b == 0), stop=True, skip_group_check=True)
                mm.then_inc(sum_used, 1)

            def spread(n):
                pe.wait_ge(diag_done, n + 1)
                pe.matmul(ps[:, r_bank(n), :], ones, diag[:, n % 2, :], start=True, stop=True
                          ).then_inc(r_ready, 1)

            def gate_up(z, i, f, h, new_input):
                n = 4 * ITERS * z + i * 4 + (2 * f + h)
                if not isinstance(n, int) or n >= 2:
                    pe.wait_ge(uf_done, n - 1)
                for j in range(2):
                    s = (W_FFN[z] + 2 * f + j) % SPLIT
                    if h == 0:
                        pe.wait_ge(lo_split, i * CPI + (W_FFN[z] + 2 * f + j + 1))
                    for k in range(KC):
                        if new_input and j == 0:
                            pe.wait_ge(n_lo, NORM_AT[2 * z] + KC * h + k + 1)
                        if z == 1 and new_input and h == 0 and j == 1:
                            if k == 0:
                                total(2, 1)
                            if k == 4:
                                spread(STD_AT[2] + 1)
                        mm = product(ps[:, 2 * h + j, :], w_hi[:, s, blk(k)], w_lo[:, s, blk(k)],
                                     h_hi[:, k, half(h)], h_lo[:, k, half(h)], k == 0, k == KC - 1)
                mm.then_inc(gu_ready, 1)

            def down(z, i, h, d):
                n = X_AT[z] + i * 16 + (KC * h + d)
                if not isinstance(n, int) or n >= 4:
                    pe.wait_ge(x_added, n - 3)
                for f in range(FPI):
                    s = (W_FFN[z] + 2 * FPI + f) % SPLIT
                    mm = product(ps[:, 4 + d % 4, :], w_hi[:, s, blk(d)], w_lo[:, s, blk(d)],
                                 u_hi[:, f, half(h)], u_lo[:, f, half(h)], f == 0, f == FPI - 1)
                mm.then_inc(y_ready, 1)

            def ffn_step(z, i, first=False, last=False):
                for f in range(FPI):
                    for h in range(NH2):
                        gate_up(z, i, f, h, first and f == 0)
                pe.wait_ge(lo_split, i * CPI + (W_FFN[z] + CPI))
                for h in range(NH2):
                    pe.wait_ge(u_lo_done, 4 * ITERS * z + i * 4 + (3 + h))
                    for d in range(KC):
                        down(z, i, h, d)
                        if last and h == 1 and d == 3:
                            total(2 * z + 1, 0)
                        if last and h == 1 and d == 5:
                            spread(STD_AT[2 * z + 1])
                if last:
                    total(2 * z + 1, 1)

            def ffn(z):
                ffn_step(z, 0, first=True)
                with nc.tensor.Fori(1, ITERS - 1) as i:
                    ffn_step(z, i)
                ffn_step(z, ITERS - 1, last=True)

            def free_bank(p):
                if p >= 4:
                    vector, n = evacuated(p - 4)
                    pe.wait_ge(dve_emptied if vector else act_emptied, n)

            def mixer_in():
                for m in range(N_IN):
                    s = (W_IN + m) % SPLIT
                    pe.wait_ge(lo_split, W_IN + m + 1)
                    for h in range(NH2):
                        p = 2 * m + h
                        free_bank(p)
                        for k in range(KC):
                            if m == 0:
                                pe.wait_ge(n_lo, NORM_AT[1] + KC * h + k + 1)
                            mm = product(ps[:, 4 + p % 4, :], w_hi[:, s, blk(k)], w_lo[:, s, blk(k)],
                                         h_hi[:, k, half(h)], h_lo[:, k, half(h)], k == 0, k == KC - 1)
                        mm.then_inc(tile_ready, 1)
                        if p == 0:
                            spread(STD_AT[1] + 1)
                        if p in (2 * VA, 2 * QA):
                            n = LAT_STD_AT + (0 if p == 2 * VA else 2)
                            spread(n)
                            spread(n + 1)
                    if m == KA:
                        stats(LAT_AT, 1, 0)
                        stats(LAT_AT + 1, 1, 2)
                        stats(LAT_AT + 2, 2, 1)
                        stats(LAT_AT + 4, 2, 3)
                    if m == QA:
                        pe.wait_ge(act_emptied, evacuated(2 * VA + 1)[1])
                        pe.wait_ge(t_done, LAT_AT + 4)
                        for b in range(NBLK):
                            tr = pe.transpose(ps[:, b // 4, blk(b % 4)], vT[:, blk(b)], ident)
                            if b % 4 == 3:
                                tr.then_inc(vt_ready, 1)

            def latent_products():
                s_kv = W_UKV % SPLIT
                s_q = [(W_UQ + k) % SPLIT for k in range(2)]
                pe.wait_ge(lo_split, W_UKV + 1)
                pe.wait_ge(n_lo, LAT_AT + 6)
                for p in range(MLA_FIRST, len(TILES)):
                    what, m, h = TILES[p]
                    free_bank(p)
                    out_p = ps[:, 4 + p % 4, :]
                    if what == "knope":
                        mm = product(out_p, w_hi[:, s_kv, blk(m)], w_lo[:, s_kv, blk(m)],
                                     kv_hi[:, half(h)], kv_lo[:, half(h)], True, True)
                    elif what == "v":
                        mm = product(out_p, kv_hi[:, blk(h)], kv_lo[:, blk(h)],
                                     w_hi[:, s_kv, HALF:D], w_lo[:, s_kv, HALF:D], True, True)
                    else:
                        col = {"qnope": m, "rope": 4 + m, "swapped": 6 + m}[what]
                        for k in range(2):
                            mm = product(out_p, w_hi[:, s_q[k], blk(col)], w_lo[:, s_q[k], blk(col)],
                                         q_hi[:, k, half(h)], q_lo[:, k, half(h)], k == 0, k == 1)
                    mm.then_inc(tile_ready, 1)

            def scores(u):
                kind, a, i = UNITS[u]
                if u >= 2:
                    if UNITS[u - 2][0] == "mla":
                        pe.wait_ge(exp_done, u - 1)
                    else:
                        pe.wait_ge(biased, sum(v[0] == "swa" for v in UNITS[:u - 1]))
                b0 = 2 * (u % 2)
                if kind == "mla":
                    r = ROPE * (a % 2)
                    for lo in range(0, (i + 1) * P, HALF):
                        hi = min(lo + HALF, (i + 1) * P)
                        bank = ps[:, b0 + lo // HALF, :]
                        pe.matmul(bank[:, 0:hi - lo], o_all[:, 4 + a, blk(i)], k_nope[:, a, lo:hi],
                                  start=True, stop=False)
                        mm = pe.matmul(bank[:, 0:hi - lo], q_r[r:r + ROPE, a // 2, blk(i)],
                                       k_r[r:r + ROPE, lo:hi], start=False, stop=(hi <= i * P))
                        if hi > i * P:
                            mm = pe.matmul(bank[:, i * P - lo:hi - lo], ident, mask, start=False, stop=True)
                else:
                    lo, w = max(i - 1, 0) * P, P if i == 0 else 2 * P
                    for c in range(2):
                        for g in range(2):
                            rows = slice(SWA_DIM * g, SWA_DIM * g + SWA_DIM)
                            mm = pe.matmul(ps[:, b0 + g, c * w:c * w + w], o_all[rows, 2 * a + c, blk(i)],
                                           k_a[rows, lo:lo + w], start=True, stop=True)
                mm.then_inc(s_ready, 1)

            def turn(u):
                kind, _, i = UNITS[u]
                pe.wait_ge(p_done, u + 1)
                if u >= 1:
                    pe.wait_ge(pt_act, u)
                    pe.wait_ge(pt_dve, sum(pt_cols(v) > HALF for v in range(u)))
                if kind == "mla":
                    moves = [(j, j * P) for j in range(i + 1)]
                else:
                    kbs = 1 if i == 0 else 2
                    moves = [(kb * SWA_GROUP + c, (c * kbs + kb) * P)
                             for kb in range(kbs) for c in range(SWA_GROUP)]
                for j, lo in moves:
                    tr = pe.transpose(ps[:, 4 + j // 4, blk(j % 4)], p_sb[:, u % P_SLOTS, lo:lo + P], ident)
                tr.then_inc(pt_ready, 1)

            def values(u):
                kind, a, i = UNITS[u]
                pe.wait_ge(pt_act, u + 1)
                pe.wait_ge(pt_dve, sum(pt_cols(v) > HALF for v in range(u + 1)))
                if u >= 2:
                    pe.wait_ge(o_done, u - 1)
                if kind == "mla":
                    for j in range(i + 1):
                        mm = pe.matmul(ps[:, 6 + u % 2, 0:P], v_b[:, j, blk(a)], pt_sb[:, u % 2, blk(j)],
                                       start=(j == 0), stop=(j == i))
                else:
                    keys = [0] if i == 0 else [i - 1, i]
                    for n, b in enumerate(keys):
                        for g in range(2):
                            rows = slice(SWA_DIM * g, SWA_DIM * g + SWA_DIM)
                            lo = n * HALF + g * 2 * P
                            mm = pe.matmul(ps[rows, 6 + u % 2, 0:2 * P], v_a[:, b, rows],
                                           pt_sb[:, u % 2, lo:lo + 2 * P], start=(n == 0),
                                           stop=(n == len(keys) - 1))
                mm.then_inc(o_ready, 1)

            def attention():
                pe.wait_ge(act_emptied, N_ACT)
                pe.wait_ge(dve_emptied, N_DVE)
                pe.wait_ge(rope_done, 4)
                pe.wait_ge(va_done, 2)
                for u in range(NU + 3):
                    if u < NU:
                        scores(u)
                    if 2 <= u < NU + 2:
                        turn(u - 2)
                    if u >= 3:
                        values(u - 3)

            def mixer_out():
                for d in range(KC):
                    s = (W_OUT + d) % SPLIT
                    pe.wait_ge(lo_split, W_OUT + d + 1)
                    for h in range(NH2):
                        w = 2 * d + h
                        if w >= 4:
                            pe.wait_ge(x_added, X_MIX + w - 3)
                        for k in range(KC):
                            if d == 0:
                                pe.wait_ge(o_lo, KC * h + k + 1)
                            mm = product(ps[:, 4 + w % 4, :], w_hi[:, s, blk(k)], w_lo[:, s, blk(k)],
                                         h_hi[:, k, half(h)], h_lo[:, k, half(h)], k == 0, k == KC - 1)
                        mm.then_inc(y_ready, 1)
                total(2, 0)
                spread(STD_AT[2])

            pe.wait_ge(const_landed, 16)
            stats(NORM_AT[0], KC, r_bank(0))
            stats(NORM_AT[0] + KC, KC, r_bank(1))
            spread(0)
            spread(1)
            pe.wait_ge(oh_landed, 16)
            pe.wait_ge(rel_landed, 16)
            pe.matmul(ps[0:SWA_HEADS, 7, 0:LINE], rel[:], onehot[:], start=True, stop=True
                      ).then_inc(line_ready, 1)
            ffn(0)
            mixer_in()
            latent_products()
            attention()
            mixer_out()
            ffn(1)
            spread(STD_AT[3] + 1)

        def squares_used(n):
            if n < NORM_AT[1]:
                return stat_done, n + 1
            if LAT_AT <= n < NORM_AT[2]:
                return stat_done, NORM_AT[1] + n - LAT_AT + 1
            s = 1 if n < LAT_AT else 2 if n < NORM_AT[3] else 3
            h, c = divmod(n - NORM_AT[s], KC)
            return summed, (KC - 1) * (NH2 * (s - 1) + h) + max(c, 1)

        def chunk_free(n):
            m = n - W_IN
            if m < -2:
                return gu_ready, 4 * ITERS - (0 if m >= -4 else 2)
            if m < 0:
                return y_ready, X_MIX
            if m < N_IN:
                return tile_ready, 2 * m + 2
            if n < W_UKV:
                return tile_ready, len(TILES)
            if n == W_UKV:
                return tile_ready, MLA_FIRST + 16
            return y_ready, X_MIX + 2 * (n - W_OUT) + 2

        @block.scalar
        def _(act):
            def hi_part(base, i, k, free):
                act.wait_ge(raw_landed[(base + k) % RAW], i * (16 * CPI // RAW) + 16 * ((base + k) // RAW + 1))
                if free is not None:
                    act.wait_ge(*free)
                act.activation(w_hi[:, (base + k) % SPLIT, :], w_raw[:, (base + k) % RAW, :], ACT.Copy
                               ).then_inc(hi_split, 1)

            def hi_of(n):
                hi_part(n, 0, 0, chunk_free(n - SPLIT))

            def square(n, source, ready):
                if ready is not None:
                    act.wait_ge(*ready)
                if n - 2 >= 0:
                    act.wait_ge(*squares_used(n - 2))
                act.activation(sq[:, n % 2, :], source, ACT.Square).then_inc(sq_done, 1)

            def deviation(n, size, sums):
                act.wait_ge(*sums)
                if n >= 4:
                    act.wait_ge(rstd_done, n - 3)
                act.activation(std[:, n % 4, :], ps[:, r_bank(n), 0:4], ACT.Sqrt, bias=eps[:, 0:1],
                               scale=1.0 / size).then_inc(std_done, 1)

            def shifted(s, h, c):
                n = NORM_AT[s] + KC * h + c
                act.wait_ge(t_done, n + 1)
                act.activation(h_hi[:, c, half(h)], tt[:, n % 2, :], ACT.Identity,
                               bias=mod[:, 3 * KC * s + c:3 * KC * s + c + 1]).then_inc(n_hi, 1)

            def norm(s, tile_at):
                for c in range(KC):
                    square(NORM_AT[s] + c, x[:, c, half(0)], tile_at(0, c))
                deviation(STD_AT[s], D, (sum_used, NH2 * (s - 1) + 1))
                for c in range(KC):
                    if s < 3:
                        shifted(s, 0, c)
                    square(NORM_AT[s] + KC + c, x[:, c, half(1)], tile_at(1, c))
                deviation(STD_AT[s] + 1, D, (sum_used, NH2 * (s - 1) + 2))
                if s < 3:
                    for c in range(KC):
                        shifted(s, 1, c)

            def first_norm():
                for h in range(NH2):
                    for c in range(KC):
                        square(KC * h + c, x[:, c, half(h)], (x_landed[h], 16))
                    deviation(h, D, (stat_done, KC * h + KC))
                for h in range(NH2):
                    for k in range(2 * h, 2 * h + 2):
                        hi_part(k, 0, 0, None)
                    for c in range(KC):
                        shifted(0, h, c)
                act.wait_ge(line_added, 1)
                act.dma_start(line_dram.ap().rearrange("q h t -> h q t"), line[:].rearrange(
                    "h (q t) -> h q t", q=1).broadcast_to([SWA_HEADS, P, LINE])).then_inc(line_saved, 16)

            def silu(z, i, f, h):
                n = 4 * ITERS * z + i * 4 + (2 * f + h)
                act.wait_ge(gu_ready, n + 1)
                if not isinstance(n, int) or n >= 2:
                    act.wait_ge(uf_done, n - 1)
                act.activation(sil[:, h, :], ps[:, 2 * h, :], ACT.Silu).then_inc(sil_done, 1)

            def u_hi_part(z, i, f, h):
                act.wait_ge(uf_done, 4 * ITERS * z + i * 4 + (2 * f + h + 1))
                act.activation(u_hi[:, f, half(h)], uf[:, h, :], ACT.Copy).then_inc(u_hi_done, 1)

            def ffn_step(z, i, first=False, last=False):
                w = W_FFN[z]
                after = 4 * ITERS * z + i * 4
                silu(z, i, 0, 0)
                if z == 0 and first:
                    act.wait_ge(line_saved, 16)
                u_hi_part(z, i, 0, 0)
                for k in (4, 5):
                    n = X_AT[z] + i * 16
                    free = (y_ready, n) if not isinstance(n, int) or n > 0 else None
                    hi_part(w, i, k, free)
                silu(z, i, 0, 1)
                u_hi_part(z, i, 0, 1)
                more = not (last and z == 1)
                for k in (0, 1) if more else ():
                    hi_part(w + CPI, i, k, (gu_ready, after + 2))
                silu(z, i, 1, 0)
                u_hi_part(z, i, 1, 0)
                silu(z, i, 1, 1)
                u_hi_part(z, i, 1, 1)
                for k in (2, 3) if more else ():
                    hi_part(w + CPI, i, k, (gu_ready, after + 4))

            def ffn(z):
                ffn_step(z, 0, first=True)
                with nc.scalar.Fori(1, ITERS - 1) as i:
                    ffn_step(z, i)
                ffn_step(z, ITERS - 1, last=True)
                tile = X_AT[z] + 16 * (ITERS - 1)
                norm(2 * z + 1, lambda h, c: (x_added, tile + KC * h + c + 1))

            def empty(p):
                what, m, h = TILES[p]
                if by_vector(p):
                    return
                if what == "in":
                    to = {KV: kvl[:, half(h)], Q0: ql[:, 0, half(h)], Q1: ql[:, 1, half(h)],
                          KA: k_a[:, half(h)], VA: vT[:, half(h)]}.get(m)
                    if to is None:
                        to = o_all[:, m - QA, half(h)]
                elif what == "knope":
                    to = k_nope[:, m, half(h)]
                else:
                    to = o_all[:, 4 + m, half(h)]
                act.wait_ge(tile_ready, p + 1)
                act.activation(to, ps[:, 4 + p % 4, :], ACT.Copy).then_inc(act_emptied, 1)

            def latent_square(v):
                source = (kvl[:, half(v)] if v < 2 else ql[:, v % 2, half((v - 2) // 2)])
                square(LAT_AT + v, source, (act_emptied, evacuated(2 * Q1 + 1)[1]))

            def latent_hi(v):
                to = kv_hi[:, half(v)] if v < 2 else q_hi[:, v % 2, half((v - 2) // 2)]
                if v == 0:
                    act.wait_ge(x_saved, 16)
                act.wait_ge(t_done, LAT_AT + v + 1)
                act.activation(to, tt[:, (LAT_AT + v) % 2, :], ACT.Copy).then_inc(n_hi, 1)

            def mixer_in():
                hi_of(W_IN + 4)
                for m in range(N_IN):
                    empty(2 * m)
                    hi_of(W_IN + m + 5)
                    empty(2 * m + 1)
                    if m == Q1:
                        latent_square(0)
                        latent_square(1)
                    if m == KA:
                        for v in range(2, 6):
                            latent_square(v)
                        for j, (tiles, size) in enumerate(
                                [(1, KV_RANK), (2, KV_RANK), (4, Q_RANK), (6, Q_RANK)]):
                            deviation(LAT_STD_AT + j, size, (stat_done, NORM_AT[1] + tiles))
                    if VA <= m <= VA + 2:
                        latent_hi(2 * (m - VA))
                        latent_hi(2 * (m - VA) + 1)
                    if m == QA:
                        for j in range(2):
                            act.wait_ge(vt_ready, j + 1)
                            act.activation(v_a[:, 4 * j:4 * j + 4, :], ps[:, j, :].rearrange(
                                "p (b d) -> p b d", b=4), ACT.Copy).then_inc(va_done, 1)

            def exps(u):
                kind, a, i = UNITS[u]
                s = u % 2
                act.wait_ge(max_done, u + 1)
                p_u = p_sb[:, u % P_SLOTS, :]
                if kind == "mla":
                    if u >= P_SLOTS:
                        act.wait_ge(pt_ready, u - P_SLOTS + 1)
                    w = (i + 1) * P
                    act.activation(p_u[:, 0:w], ps[:, 2 * s:2 * s + 2, :].rearrange("p b c -> p (b c)")[:, 0:w],
                                   ACT.Exp, bias=negm[:, s, 0:1], scale=MLA_SCALE,
                                   accum_out=den[:, s, 0:1]).then_inc(exp_done, 1)
                else:
                    w = P if i == 0 else 2 * P
                    for c in range(SWA_GROUP):
                        act.activation(p_u[:, c * w:(c + 1) * w], p_u[:, c * w:(c + 1) * w], ACT.Exp,
                                       bias=negm[:, s, c:c + 1], accum_out=den[:, s, c:c + 1])
                    act.activation(esink[:, s, :], dsink[:, s, :], ACT.Exp).then_inc(exp_done, 1)

            def copy_turned(u):
                act.wait_ge(pt_ready, u + 1)
                if u >= 2:
                    act.wait_ge(o_ready, u - 1)
                w = min(pt_cols(u), HALF)
                act.activation(pt_sb[:, u % 2, 0:w], ps[:, 4, 0:w], ACT.Copy).then_inc(pt_act, 1)

            def copy_output(u):
                kind, a, i = UNITS[u]
                act.wait_ge(o_ready, u + 1)
                if kind == "mla":
                    act.activation(o_all[:, 4 + a, blk(i)], ps[:, 6 + u % 2, 0:P], ACT.Copy).then_inc(o_done, 1)
                else:
                    act.activation(o_all[:, 2 * a:2 * a + 2, blk(i)],
                                   ps[:, 6 + u % 2, 0:2 * P].rearrange("p (c q) -> p c q", c=2),
                                   ACT.Copy).then_inc(o_done, 1)

            def attention():
                for u in range(NU + 3):
                    if u < NU:
                        exps(u)
                    if 2 <= u < NU + 2:
                        copy_turned(u - 2)
                    if u >= 3:
                        copy_output(u - 3)

            def mixer_out():
                act.wait_ge(o_done, NU)
                for h in range(NH2):
                    for c in range(KC):
                        act.activation(h_hi[:, c, half(h)], o_all[:, c, half(h)], ACT.Copy).then_inc(o_hi, 1)
                for d in range(1, 7):
                    hi_of(W_OUT + d + 5)

            act.dma_start(c_act[:], c_in).then_inc(c_landed, 16)
            act.dma_start(small[:], small_in).then_inc(small_landed, 16)
            act.dma_start(consts[:], const_in).then_inc(const_landed, 16)
            act.dma_start(sinks[:], sinks_in).then_inc(sinks_landed, 16)
            act.dma_start(onehot[:], oh_in).then_inc(oh_landed, 16)
            act.dma_start(rel[:], rel_in).then_inc(rel_landed, 16)
            act.dma_start(linemask[:], lm_in).then_inc(lm_landed, 16)
            act.wait_ge(c_landed, 16)
            act.activation(c_act[:], c_act[:], ACT.Silu).then_inc(c_ready, 1)
            act.wait_ge(eps_ready, 1)
            first_norm()
            ffn(0)
            mixer_in()
            for p in range(MLA_FIRST, len(TILES)):
                empty(p)
            for n in range(W_OUT + 2, W_OUT + 6):
                hi_of(n)
            attention()
            mixer_out()
            norm(2, lambda h, c: (x_added, X_MIX + 2 * c + h + 1))
            ffn(1)

        @block.vector
        def _(dve):
            count = {}

            def step(ins, signal):
                count[signal.name] = count.get(signal.name, 0) + 1
                ins.then_inc(signal, 1)
                dve.wait_ge(signal, count[signal.name])

            def modulation(j):
                for k in range(4):
                    dve.wait_ge(mod_landed[k], j * 16 + 16)
                    if not isinstance(j, int) or j > 0:
                        dve.wait_ge(mod_ready, j)
                    dve.tensor_tensor_reduce(out=mod_raw[:, k, :], in0=mod_raw[:, k, :], in1=c_act[:],
                                             scale=1.0, scalar=0.0, op0=ALU.mult, op1=ALU.add,
                                             accum_out=mod_acc[:, k:k + 1]).then_inc(mod_used, 1)
                dve.wait_ge(mod_used, j * 4 + 4)
                dve.tensor_tensor(mod[:, bass.ds(j * 4, 4)], mod_acc[:], small[:, bass.ds(j * 4, 4)],
                                  ALU.add).then_inc(mod_ready, 1)

            def scale_vector(s):
                dve.wait_ge(mod_ready, 6 * s + 4)
                c0 = 3 * KC * s + KC
                dve.scalar_tensor_tensor(out=scale_v[:, s, :], in0=mod[:, c0:c0 + KC], scalar=1.0,
                                         in1=gain(s), op0=ALU.add, op1=ALU.mult).then_inc(vec_ready, 1)

            def gate_vector(s):
                dve.wait_ge(mod_ready, 6 * s + 6)
                c0 = 3 * KC * s + 2 * KC
                dve.tensor_scalar(gate_v[:, s, :], mod[:, c0:c0 + KC], 1.0 if s == 1 else 0.5, None,
                                  ALU.mult).then_inc(vec_ready, 1)

            def lo_part(base, i, k):
                dve.wait_ge(hi_split, i * CPI + (base + k + 1))
                s = (base + k) % SPLIT
                dve.tensor_tensor(w_lo[:, s, :], w_raw[:, (base + k) % RAW, :], w_hi[:, s, :].bitcast(F32),
                                  ALU.subtract).then_inc(lo_split, 1)

            def lo_of(n):
                lo_part(n, 0, 0)

            def invert(n):
                dve.wait_ge(std_done, n + 1)
                dve.reciprocal(rstd[:, n % 4, :], std[:, n % 4, :]).then_inc(rstd_done, 1)
                dve.wait_ge(rstd_done, n + 1)
                if n >= 2:
                    dve.wait_ge(r_ready, n - 1)
                dve.tensor_tensor(diag[:, n % 2, :].rearrange("p (b t) -> p b t", b=4),
                                  ident.rearrange("p (b t) -> p b t", b=1).broadcast_to([P, 4, P]),
                                  rstd[:, n % 4, :].rearrange("p (b t) -> p b t", t=1).broadcast_to([P, 4, P]),
                                  ALU.mult).then_inc(diag_done, 1)

            def scaled(n, source, scale, r):
                dve.wait_ge(r_ready, r + 1)
                if n >= 2:
                    dve.wait_ge(n_lo, n - 1)
                dve.scalar_tensor_tensor(out=tt[:, n % 2, :], in0=source, scalar=scale, in1=ps[:, r_bank(r), :],
                                         op0=ALU.mult, op1=ALU.mult).then_inc(t_done, 1)

            def shifted_lo(s, h, c):
                n = NORM_AT[s] + KC * h + c
                dve.wait_ge(n_hi, n + 1)
                dve.scalar_tensor_tensor(out=h_lo[:, c, half(h)], in0=tt[:, n % 2, :],
                                         scalar=mod[:, 3 * KC * s + c:3 * KC * s + c + 1],
                                         in1=h_hi[:, c, half(h)].bitcast(F32), op0=ALU.add,
                                         op1=ALU.subtract).then_inc(n_lo, 1)

            def norm_half(s, h, between=lambda c: None):
                for c in range(KC + 1):
                    if c < KC:
                        scaled(NORM_AT[s] + KC * h + c, x[:, c, half(h)], scale_v[:, s, c:c + 1], STD_AT[s] + h)
                    if c >= 1:
                        shifted_lo(s, h, c - 1)
                    between(c)
                if h == 0 and s > 0:
                    invert(STD_AT[s] + 1)

            def final_half(h, between=lambda c: None):
                dve.wait_ge(r_ready, STD_AT[3] + h + 1)
                for c in range(KC):
                    dve.scalar_tensor_tensor(out=x[:, c, half(h)], in0=x[:, c, half(h)],
                                             scalar=gain(3)[:, c:c + 1], in1=ps[:, r_bank(STD_AT[3] + h), :],
                                             op0=ALU.mult, op1=ALU.mult).then_inc(out_ready, 1)
                    between(c)

            def multiply(z, i, f, h):
                n = 4 * ITERS * z + i * 4 + (2 * f + h)
                dve.wait_ge(sil_done, n + 1)
                if not isinstance(n, int) or n >= 2:
                    dve.wait_ge(u_lo_done, n - 1)
                dve.tensor_tensor(uf[:, h, :], sil[:, h, :], ps[:, 2 * h + 1, :], ALU.mult).then_inc(uf_done, 1)
                dve.wait_ge(u_hi_done, n + 1)
                dve.tensor_tensor(u_lo[:, f, half(h)], uf[:, h, :], u_hi[:, f, half(h)].bitcast(F32),
                                  ALU.subtract).then_inc(u_lo_done, 1)

            def add(n, bank, d, h, s):
                dve.wait_ge(y_ready, n + 1)
                dve.scalar_tensor_tensor(out=x[:, d, half(h)], in0=ps[:, bank, :], scalar=gate_v[:, s, d:d + 1],
                                         in1=x[:, d, half(h)], op0=ALU.mult, op1=ALU.add).then_inc(x_added, 1)

            def ffn_step(z, i, first=False, last=False):
                w = W_FFN[z]
                more = not (last and z == 1)
                multiply(z, i, 0, 0)
                for k in (4, 5):
                    lo_part(w, i, k)
                if z == 0:
                    modulation(4 if first else i + 6)
                multiply(z, i, 0, 1)
                if z == 0 and first:
                    modulation(5)
                    gate_vector(0)
                    dve.wait_ge(vec_ready, 2)
                if z == 0 and last:
                    modulation(MODC // 4 - 1)
                    for s in (1, 2):
                        scale_vector(s)
                        gate_vector(s)
                    dve.wait_ge(vec_ready, 6)
                for k in (0, 1) if more else ():
                    lo_part(w + CPI, i, k)
                multiply(z, i, 1, 0)
                if z == 0 and first:
                    modulation(6)
                multiply(z, i, 1, 1)

                def added(h, d):
                    add(X_AT[z] + i * 16 + (KC * h + d), 4 + d % 4, d, h, 2 * z)

                for d in range(KC):
                    added(0, d)
                    if d in (1, 3) and more:
                        lo_part(w + CPI, i, 2 + d // 2)
                if not last:
                    for d in range(KC):
                        added(1, d)
                    return
                for d in range(6):
                    added(1, d)
                    if d == 4:
                        invert(STD_AT[2 * z + 1])

                def between(c):
                    if 6 + c < KC:
                        added(1, 6 + c)

                if z == 0:
                    norm_half(1, 0, between)
                    norm_half(1, 1)
                else:
                    final_half(0, between)
                    invert(STD_AT[3] + 1)
                    final_half(1)

            def ffn(z):
                ffn_step(z, 0, first=True)
                with nc.vector.Fori(1, ITERS - 1) as i:
                    ffn_step(z, i)
                ffn_step(z, ITERS - 1, last=True)

            def rotate_key(h):
                p = 2 * KROPE + h
                bank = ps[:, 4 + p % 4, :]
                if h == 0:
                    dve.wait_ge(tab_landed, 16)
                dve.wait_ge(tile_ready, p + 1)
                r = slice(0, ROPE)
                dve.tensor_tensor(tt[r, 0, :], bank[r, :], tab[r, 0, half(h)], ALU.mult)
                step(dve.tensor_tensor(tt[r, 1, :], bank[ROPE:P, :], tab[ROPE:P, 1, half(h)], ALU.mult),
                     rope_part)
                dve.tensor_tensor(k_r[r, half(h)], tt[r, 0, :], tt[r, 1, :], ALU.add)
                dve.tensor_tensor(k_r[ROPE:P, half(h)], tt[r, 0, :], tt[r, 1, :], ALU.add
                                  ).then_inc(dve_emptied, 1)
                dve.wait_ge(dve_emptied, h + 1)

            def rotate_query(p):
                _, r, h = TILES[p]
                dve.wait_ge(tile_ready, p + 2)
                dve.tensor_tensor(tt[:, 0, :], ps[:, 4 + p % 4, :], tab[:, 0, half(h)], ALU.mult
                                  ).then_inc(dve_emptied, 1)
                dve.tensor_tensor(tt[:, 1, :], ps[:, 4 + (p + 1) % 4, :], tab[:, 1, half(h)], ALU.mult
                                  ).then_inc(dve_emptied, 1)
                dve.wait_ge(dve_emptied, evacuated(p + 1)[1])
                step(dve.tensor_tensor(q_r[:, r, half(h)], tt[:, 0, :], tt[:, 1, :], ALU.add), rope_done)

            def latent(v):
                h = v if v < 2 else (v - 2) // 2
                source = kvl[:, half(h)] if v < 2 else ql[:, v % 2, half(h)]
                g = lat_gain[:, 2:3] if v < 2 else lat_gain[:, v % 2:v % 2 + 1]
                r = LAT_STD_AT + (h if v < 2 else 2 + h)
                scaled(LAT_AT + v, source, g, r)

            def latent_lo(v):
                h = v if v < 2 else (v - 2) // 2
                hi, lo = (kv_hi[:, half(h)], kv_lo[:, half(h)]) if v < 2 else (
                    q_hi[:, v % 2, half(h)], q_lo[:, v % 2, half(h)])
                dve.wait_ge(n_hi, LAT_AT + v + 1)
                dve.tensor_tensor(lo, tt[:, (LAT_AT + v) % 2, :], hi.bitcast(F32), ALU.subtract
                                  ).then_inc(n_lo, 1)

            def mixer_in():
                lo_of(W_IN + 4)
                for m in range(N_IN):
                    lo_of(W_IN + m + 5)
                    if m == KROPE:
                        rotate_key(0)
                        rotate_key(1)
                    if m == KA:
                        invert(LAT_STD_AT)
                        invert(LAT_STD_AT + 1)
                    if m == VA:
                        latent(0)
                        latent(1)
                        invert(LAT_STD_AT + 2)
                        invert(LAT_STD_AT + 3)
                    if VA <= m <= VA + 2:
                        v = 2 * (m - VA)
                        latent_lo(v)
                        latent_lo(v + 1)
                        if v < 4:
                            latent(v + 2)
                            latent(v + 3)

            def empty_value(p):
                dve.wait_ge(tile_ready, p + 1)
                dve.tensor_copy(v_b[:, TILES[p][2], :], ps[:, 4 + p % 4, :]).then_inc(dve_emptied, 1)

            def latent_products():
                for p in range(MLA_FIRST, len(TILES)):
                    if TILES[p][0] == "v":
                        empty_value(p)
                    if TILES[p][0] == "rope":
                        rotate_query(p)
                for n in range(W_OUT + 2, W_OUT + 6):
                    lo_of(n)

            def maxima(u):
                kind, a, i = UNITS[u]
                s = u % 2
                dve.wait_ge(s_ready, u + 1)
                scores = ps[:, 2 * s:2 * s + 2, :].rearrange("p b c -> p (b c)")
                if kind == "mla":
                    step(dve.tensor_reduce(mx[:, s, 0:1], scores[:, 0:(i + 1) * P], AX.X, ALU.max), max_part)
                    dve.tensor_scalar(negm[:, s, 0:1], mx[:, s, 0:1], -MLA_SCALE, None, ALU.mult
                                      ).then_inc(max_done, 1)
                    return
                w = P if i == 0 else 2 * P
                if u >= P_SLOTS:
                    dve.wait_ge(pt_ready, u - P_SLOTS + 1)
                heads = slice(SWA_GROUP * a, SWA_GROUP * a + SWA_GROUP)
                p4 = p_sb[:, u % P_SLOTS, 0:SWA_GROUP * w].rearrange("p (c k) -> p c k", c=SWA_GROUP)
                for g in range(2):
                    ins = dve.scalar_tensor_tensor(
                        out=p4[:, 2 * g:2 * g + 2, :], in0=ps[:, 2 * s + g, 0:2 * w].rearrange(
                            "p (c k) -> p c k", c=2), scalar=SWA_SCALE,
                        in1=bias[:, SWA_GROUP * a + 2 * g:SWA_GROUP * a + 2 * g + 2, 2 * P - w:2 * P],
                        op0=ALU.mult, op1=ALU.add)
                step(ins, biased)
                step(dve.tensor_reduce(mx[:, s, :], p4, AX.X, ALU.max), max_part)
                step(dve.tensor_tensor(mx[:, s, :], mx[:, s, :], sinks[:, heads], ALU.max), max_part)
                dve.tensor_scalar(negm[:, s, :], mx[:, s, :], -1.0, None, ALU.mult)
                dve.tensor_tensor(dsink[:, s, :], sinks[:, heads], mx[:, s, :], ALU.subtract
                                  ).then_inc(max_done, 1)

            def normalise(u):
                kind, a, i = UNITS[u]
                s = u % 2
                p_u = p_sb[:, u % P_SLOTS, :]
                dve.wait_ge(exp_done, u + 1)
                if kind == "mla":
                    w = (i + 1) * P
                    step(dve.reciprocal(rden[:, s, 0:1], den[:, s, 0:1]), den_part)
                    dve.tensor_scalar(p_u[:, 0:w], p_u[:, 0:w], rden[:, s, 0:1], None, ALU.mult
                                      ).then_inc(p_done, 1)
                    return
                w = P if i == 0 else 2 * P
                step(dve.tensor_tensor(den[:, s, :], den[:, s, :], esink[:, s, :], ALU.add), den_part)
                step(dve.reciprocal(rden[:, s, :], den[:, s, :]), den_part)
                for c in range(SWA_GROUP):
                    ins = dve.tensor_scalar(p_u[:, c * w:(c + 1) * w], p_u[:, c * w:(c + 1) * w],
                                            rden[:, s, c:c + 1], None, ALU.mult)
                ins.then_inc(p_done, 1)

            def copy_turned(u):
                w = pt_cols(u) - HALF
                if w <= 0:
                    return
                dve.wait_ge(pt_ready, u + 1)
                if u >= 2:
                    dve.wait_ge(o_ready, u - 1)
                dve.tensor_copy(pt_sb[:, u % 2, HALF:HALF + w], ps[:, 5, 0:w]).then_inc(pt_dve, 1)

            def attention():
                dve.wait_ge(sinks_landed, 16)
                dve.wait_ge(bias_landed, 16)
                for u in range(NU + 2):
                    if u < NU:
                        maxima(u)
                    if 1 <= u <= NU:
                        normalise(u - 1)
                    if u >= 2:
                        copy_turned(u - 2)

            def mixer_out():
                for h in range(NH2):
                    for c in range(KC):
                        dve.wait_ge(o_hi, KC * h + c + 1)
                        dve.tensor_tensor(h_lo[:, c, half(h)], o_all[:, c, half(h)],
                                          h_hi[:, c, half(h)].bitcast(F32), ALU.subtract).then_inc(o_lo, 1)
                dve.wait_ge(x_back, 16)
                for d in range(KC):
                    for h in range(NH2):
                        w = 2 * d + h
                        add(X_MIX + w, 4 + w % 4, d, h, 1)
                    if 1 <= d <= 6:
                        lo_of(W_OUT + d + 5)
                invert(STD_AT[2])

            dve.memset(eps[:], EPS).then_inc(eps_ready, 1)
            dve.wait_ge(small_landed, 16)
            dve.wait_ge(c_ready, 1)
            for j in range(3):
                modulation(j)
            invert(0)
            invert(1)
            modulation(3)
            scale_vector(0)
            dve.wait_ge(vec_ready, 1)
            for k in range(2):
                lo_part(k, 0, 0)
            norm_half(0, 0)
            for k in range(2, 4):
                lo_part(k, 0, 0)
            norm_half(0, 1)
            dve.wait_ge(line_ready, 1)
            dve.wait_ge(lm_landed, 16)
            dve.tensor_tensor(line[:], ps[0:SWA_HEADS, 7, 0:LINE], linemask[:], ALU.add
                              ).then_inc(line_added, 1)
            ffn(0)
            mixer_in()
            latent_products()
            attention()
            mixer_out()
            norm_half(2, 0)
            norm_half(2, 1)
            ffn(1)


def _columns(w, cols):
    return w[:, cols].reshape(-1, P, P).transpose(1, 0, 2).reshape(P, -1)


def weight_stream(np, gate1, up1, down1, w_in, w_uq, w_ukv, w_o, gate2, up2, down2):
    chunks = []

    def ffn(gate, up, down):
        for i in range(ITERS):
            fs = [slice((FPI * i + f) * P, (FPI * i + f + 1) * P) for f in range(FPI)]
            for f in fs:
                chunks.append(_columns(gate, f))
                chunks.append(_columns(up, f))
            for f in fs:
                chunks.append(down[f, :])

    ffn(gate1, up1, down1)
    r = np.arange
    q_at, k_at, v_at, ql_at, kv_at, kr_at = 0, 512, 640, 768, 1024, 1152
    rope = r(kr_at, kr_at + ROPE)
    swapped = np.concatenate([rope[ROPE // 2:], rope[:ROPE // 2]])
    for cols in ([r(kv_at, kv_at + P), r(ql_at, ql_at + P), r(ql_at + P, ql_at + 2 * P),
                  np.concatenate([rope, swapped]), r(k_at, k_at + P), r(v_at, v_at + P)]
                 + [np.concatenate([r(q_at + 64 * c, q_at + 64 * c + 64),
                                    r(q_at + 256 + 64 * c, q_at + 256 + 64 * c + 64)]) for c in range(4)]):
        chunks.append(_columns(w_in, cols))
    hd = NOPE + ROPE
    nope = np.concatenate([r(h * hd, h * hd + NOPE) for h in range(MLA_HEADS)])
    rope = [r(h * hd + NOPE, (h + 1) * hd) for h in range(MLA_HEADS)]
    swapped = [np.concatenate([c[ROPE // 2:], c[:ROPE // 2]]) for c in rope]
    cols = np.concatenate([nope, *rope, *swapped])
    for k in range(2):
        chunks.append(w_uq[k * P:(k + 1) * P, cols])
    chunks.append(w_ukv[:, np.concatenate([r(h * 256 + o, h * 256 + o + P) for o in (0, P)
                                           for h in range(MLA_HEADS)])])
    rows = np.concatenate([np.concatenate([r(64 * c, 64 * c + 64), r(256 + 64 * c, 256 + 64 * c + 64)])
                           for c in range(4)] + [r(512, 1024)])
    for d in range(KC):
        chunks.append(_columns(w_o[rows, :], slice(d * P, (d + 1) * P)))
    ffn(gate2, up2, down2)
    return np.stack(chunks)


def shape_constants(np):
    f = np.float32
    causal = np.where(np.arange(P)[None, :] > np.arange(P)[:, None], f(-1e30), f(0))
    consts = np.stack([np.eye(P, dtype=f), causal.astype(f), np.ones((P, P), f)], axis=1)
    inv = np.power(f(10000.0), -np.arange(0, ROPE, 2, dtype=f) / f(ROPE)).astype(f)
    ang = (np.arange(T, dtype=f)[:, None] * inv[None, :]).astype(f)
    cos, sin = np.cos(ang).T.astype(f), np.sin(ang).T.astype(f)
    tab = np.stack([np.concatenate([cos, cos, cos, cos]), np.concatenate([-sin, sin, -sin, sin])], axis=1)
    dist = 2 * P - 1 - np.arange(LINE)
    ok = (dist >= 0) & (dist < P)
    n = np.maximum(dist, 0)
    large = 16 + (np.log(np.maximum(n, 1).astype(f) / f(16)) / f(np.log(8.0)) * f(16)).astype(np.int32)
    bucket = np.where(n < 16, n, np.minimum(large, BUCKETS - 1))
    onehot = ((bucket[None, :] == np.arange(BUCKETS)[:, None]) & ok[None, :]).astype(f)
    linemask = np.broadcast_to(np.where(ok, f(0), f(-1e30)), (SWA_HEADS, LINE)).astype(f)
    return consts, tab, onehot, linemask


def kernel(x, c, w_mod, b_mod, norm_ffn1, ffn1_gate, ffn1_up, ffn1_down, norm_mix, w_in, q_norm, kv_norm,
           w_uq, w_ukv, sinks, w_o, norm_ffn2, ffn2_gate, ffn2_up, ffn2_down, rel_bias, norm_final):
    import numpy as np
    import concourse.bacc as bacc
    from concourse.bass_utils import run_bass_kernel_spmd

    def a(v):
        return np.asarray(v)

    def by_partition(v):
        return a(v).reshape(-1, P).T

    consts, tab, onehot, linemask = shape_constants(np)
    heads = [0, 1, 4, 5, 2, 3, 6, 7]
    arrays = {
        "xT_in": a(x)[0].T.reshape(KC, P, T).transpose(1, 0, 2),
        "c_in": np.broadcast_to(a(c)[0], (P, D)),
        "w_modT_in": a(w_mod)[0].T.reshape(MODC, P, D),
        "small_in": np.concatenate([by_partition(v) for v in (
            a(b_mod)[0], a(norm_ffn1)[0], a(norm_mix)[0], a(norm_ffn2)[0], a(norm_final), a(q_norm)[0],
            a(kv_norm)[0])], axis=1),
        "wstream_in": weight_stream(np, *(a(w)[0] for w in (
            ffn1_gate, ffn1_up, ffn1_down, w_in, w_uq, w_ukv, w_o, ffn2_gate, ffn2_up, ffn2_down))),
        "const_in": consts,
        "tab_in": tab,
        "sinks_in": np.broadcast_to(a(sinks)[0][heads], (P, SWA_HEADS)),
        "rel_in": a(rel_bias)[:, heads],
        "oh_in": onehot,
        "lm_in": linemask,
    }
    arrays = {n: np.ascontiguousarray(v) for n, v in arrays.items()}
    nc = bacc.Bacc("TRN2", target_bir_lowering=False, num_devices=1, dynamic_dma_scratch_size=4096)
    args = [nc.dram_tensor(n, v.shape, F32, kind="ExternalInput").ap() for n, v in arrays.items()]
    out = nc.dram_tensor("out", (P, KC, T), F32, kind="ExternalOutput").ap()
    build(nc, *args, out)
    r = run_bass_kernel_spmd(nc, [arrays], core_ids=[0])
    got = r.results[0]["out"]
    return got.transpose(1, 0, 2).reshape(D, T).T.reshape(1, T, D)
```

```python
from contextlib import ExitStack

import concourse.bass as bass
from concourse import mybir
from concourse.alu_op_type import AluOpType as ALU

F32 = mybir.dt.float32
F32R = mybir.dt.float32r
ACT = mybir.ActivationFunctionType
AX = mybir.AxisListType

P = 128
D = 1024
T = 1024
KC = D // P
HALF = 512
NH2 = T // HALF
D_FF = 2816
FPI = 2
ITERS = D_FF // P // FPI
N_MOD = 9
MODC = N_MOD * KC
EPS = 1e-6

SWA_HEADS = 8
SWA_GROUP = 4
SWA_DIM = 64
MLA_HEADS = 4
NOPE = 128
ROPE = 64
Q_RANK = 256
KV_RANK = 128
NBLK = T // P
BUCKETS = 32
LINE = 384
MLA_SCALE = (NOPE + ROPE) ** -0.5
SWA_SCALE = SWA_DIM ** -0.5

CPI = 3 * FPI
N_IN = 10
W_IN = CPI * ITERS
W_UQ = W_IN + N_IN
W_UKV = W_UQ + Q_RANK // P
W_OUT = W_UKV + KV_RANK // P
W_FFN = [0, W_OUT + KC]
N_CHUNKS = W_FFN[1] + CPI * ITERS
RAW, SPLIT = 3, 6
P_SLOTS = 3
GATE_AT = 2 * KC
SIDE = 4
WEIGHTS_AT = (4, 7, 10)

NORM_AT = [0, 16, 38, 54]
LAT_AT = 32
STD_AT = [0, 2, 8, 10]
LAT_STD_AT = 4
X_AT = [0, 16 * ITERS + 16]
X_MIX = 16 * ITERS
MLA_FIRST = 2 * N_IN
SMALL = MODC + 4 * KC + 3


def units():
    mla = [("mla", h, i) for i in range(NBLK) for h in range(MLA_HEADS)]
    swa = [("swa", g, i) for i in range(NBLK) for g in range(2)]
    out = []
    for n in range(16):
        out += [swa[n], mla[16 + n], mla[15 - n]]
    return out


def mixer_tiles():
    out = []
    for h in range(NH2):
        out += [("in", m, h) for m in range(SIDE)]
    for m in range(SIDE, N_IN):
        out += [("in", m, h) for h in range(NH2)]
    for h in range(NH2):
        for hd in range(MLA_HEADS):
            out += [("rope", hd, h), ("knope", hd, h), ("v", 0, MLA_HEADS * h + hd)]
    out += [("qnope", hd, h) for h in range(NH2) for hd in range(MLA_HEADS)]
    return out


OUT_TILES = [(d, h) for d in range(KC - 2) for h in range(NH2)] + [
    (d, h) for h in range(NH2) for d in range(KC - 2, KC)]
KV, Q0, Q1, KA, KROPE, VA, QA = 0, 1, 2, 3, 4, 5, 6
TILES = mixer_tiles()


def by_vector(p):
    what, m, _ = TILES[p]
    return what == "rope" or (what == "in" and m == KROPE)


def evacuated(p):
    mine = by_vector(p)
    return mine, sum(by_vector(q) == mine for q in range(p + 1))


def build(nc, xT, c_in, w_modT, small_in, wstream, const_in, tab_in, sinks_in, rel_in, oh_in, lm_in,
          out):
    ctx = ExitStack()
    with ctx:
        at = [4224]

        def sb(name, shape, dt, offset=None):
            size = 4
            for s in shape[1:]:
                size *= s
            if offset is None:
                offset = at[0]
                at[0] += (size + 31) // 32 * 32
            return nc.alloc_sbuf_tensor_at(name, shape, dt, offset=offset)

        x = sb("x", [P, KC, T], F32)
        h_at = at[0]
        h_hi = sb("h_hi", [P, KC, T], F32R)
        h_lo = sb("h_lo", [P, KC, T], F32R)
        w_raw = sb("w_raw", [P, RAW, D], F32)
        w_hi = sb("w_hi", [P, SPLIT, D], F32R)
        w_lo = sb("w_lo", [P, SPLIT, D], F32R)
        s_at = at[0]
        u_hi = sb("u_hi", [P, FPI, T], F32R)
        u_lo = sb("u_lo", [P, FPI, T], F32R)
        sil = sb("sil", [P, NH2, HALF], F32)
        uf = sb("uf", [P, NH2, HALF], F32)
        mod_raw = sb("mod_raw", [P, 4, D], F32)
        c_act = sb("c_act", [P, D], F32)
        tt = sb("tt", [P, 2, HALF], F32)
        p_at = at[0]
        sq = sb("sq", [P, 2, HALF], F32)
        diag = sb("diag", [P, 2, HALF], F32)
        acc = sb("acc", [P, 2, HALF], F32)
        small = sb("small", [P, SMALL], F32)
        consts = sb("consts", [P, 3, P], F32)
        mod = sb("mod", [P, MODC], F32)
        mod_acc = sb("mod_acc", [P, 4], F32)
        gate_acc = sb("gate_acc", [P, KC], F32)
        scale_v = sb("scale_v", [P, 3, KC], F32)
        gate_v = sb("gate_v", [P, 3, KC], F32)
        sinks = sb("sinks", [P, SWA_HEADS], F32)
        mx = sb("mx", [P, 2, 4], F32)
        negm = sb("negm", [P, 2, 4], F32)
        dsink = sb("dsink", [P, 2, 4], F32)
        esink = sb("esink", [P, 2, 4], F32)
        den = sb("den", [P, 2, 4], F32)
        rden = sb("rden", [P, 2, 4], F32)
        eps = sb("eps", [P, 1], F32)
        std = sb("std", [P, 4, 4], F32)
        rstd = sb("rstd", [P, 4, 4], F32)
        o_all = sb("o_all", [P, KC, T], F32, s_at)
        kvl = sb("kvl", [P, T], F32, s_at + 16384)
        ql = sb("ql", [P, 2, T], F32, s_at + 20480)
        vT = sb("vT", [P, T], F32, s_at + 28672)
        k_a = sb("k_a", [P, T], F32, s_at + 32768)
        v_a = sb("v_a", [P, NBLK, P], F32, s_at + 36864)
        k_r = sb("k_r", [P, T], F32, s_at + 40960)
        x_at = h_at - 32768
        q_hi = sb("q_hi", [P, 2, T], F32R, x_at)
        q_lo = sb("q_lo", [P, 2, T], F32R, x_at + 8192)
        kv_hi = sb("kv_hi", [P, T], F32R, x_at + 16384)
        kv_lo = sb("kv_lo", [P, T], F32R, x_at + 20480)
        tab = sb("tab", [P, 2, T], F32, x_at + 24576)
        k_nope = sb("k_nope", [P, MLA_HEADS, T], F32, h_at)
        v_b = sb("v_b", [P, NBLK, MLA_HEADS * P], F32, h_at + 16384)
        q_r = sb("q_r", [P, MLA_HEADS, T], F32, h_at + 32768)
        pt_sb = sb("pt_sb", [P, 2, D], F32, h_at + 57344)
        ident_r = sb("ident_r", [P, P], F32R, s_at + 45056)
        mask_r = sb("mask_r", [P, P], F32R, s_at + 45568)
        bias = sb("bias", [P, SWA_HEADS, 2 * P], F32, h_at + 49152)
        p_sb = sb("p_sb", [P, P_SLOTS, D], F32, p_at)
        line = sb("line", [SWA_HEADS, LINE], F32, s_at + 36864)
        onehot = sb("onehot", [BUCKETS, LINE], F32, s_at + 36864 + 4 * LINE)
        rel = sb("rel", [BUCKETS, SWA_HEADS], F32, s_at + 36864 + 8 * LINE)

        ident, mask, ones = (consts[:, j, :] for j in range(3))
        bmod = small[:, 0:MODC]

        def gain(s):
            return small[:, MODC + KC * s:MODC + KC * s + KC]

        lat_gain = small[:, MODC + 4 * KC:SMALL]

        ps = ctx.enter_context(nc.psum_tensor("ps", [P, 8, HALF], F32))

        x_save = nc.dram_tensor("x_save", [P, KC, T], F32).ap()
        line_dram = nc.dram_tensor("line_dram", [P, SWA_HEADS, LINE], F32)

        def sem(name):
            return ctx.enter_context(nc.semaphore(name))

        x_landed = [sem(f"x_landed{j}") for j in range(4)]
        c_landed = sem("c_landed")
        small_landed = sem("small_landed")
        const_landed = sem("const_landed")
        eps_ready = sem("eps_ready")
        sinks_landed = sem("sinks_landed")
        sum_used = sem("sum_used")
        raw_landed = [sem(f"raw_landed{j}") for j in range(RAW)]
        hi_split = sem("hi_split")
        first_lo_split = sem("first_lo_split")
        lo_split = sem("lo_split")
        first_mod_landed = [sem(f"first_mod_landed{j}") for j in range(4)]
        mod_landed = [sem(f"mod_landed{j}") for j in range(4)]
        mod_used = sem("mod_used")
        mod_ready = sem("mod_ready")
        gate_products = sem("gate_products")
        gate_summed = sem("gate_summed")
        gate_biased = sem("gate_biased")
        vec_ready = sem("vec_ready")
        c_ready = sem("c_ready")
        sq_done = sem("sq_done")
        stat_done = sem("stat_done")
        std_done = sem("std_done")
        rstd_done = sem("rstd_done")
        diag_done = sem("diag_done")
        r_ready = sem("r_ready")
        summed = sem("summed")
        t_done = sem("t_done")
        n_hi = sem("n_hi")
        n_lo = sem("n_lo")
        gu_ready = sem("gu_ready")
        sil_done = sem("sil_done")
        uf_done = sem("uf_done")
        u_hi_done = sem("u_hi_done")
        u_lo_done = sem("u_lo_done")
        y_ready = sem("y_ready")
        x_added = sem("x_added")
        x_saved = sem("x_saved")
        tab_landed = sem("tab_landed")
        oh_landed = sem("oh_landed")
        rel_landed = sem("rel_landed")
        lm_landed = sem("lm_landed")
        line_ready = sem("line_ready")
        line_added = sem("line_added")
        line_saved = sem("line_saved")
        bias_landed = sem("bias_landed")
        x_back = sem("x_back")
        tile_ready = sem("tile_ready")
        act_emptied = sem("act_emptied")
        dve_emptied = sem("dve_emptied")
        key_rotated = sem("key_rotated")
        rope_done = sem("rope_done")
        vt_ready = sem("vt_ready")
        va_done = sem("va_done")
        mask_ready = sem("mask_ready")
        s_ready = sem("s_ready")
        biased = sem("biased")
        max_part = sem("max_part")
        max_done = sem("max_done")
        exp_done = sem("exp_done")
        den_part = sem("den_part")
        p_done = sem("p_done")
        pt_ready = sem("pt_ready")
        pt_act = sem("pt_act")
        pt_dve = sem("pt_dve")
        o_ready = sem("o_ready")
        o_done = sem("o_done")
        o_hi = sem("o_hi")
        o_lo = sem("o_lo")
        out_ready = sem("out_ready")
        out_saved = sem("out_saved")

        def half(h):
            return slice(h * HALF, (h + 1) * HALF)

        def blk(i):
            return slice(i * P, (i + 1) * P)

        def lo_count(n):
            return n + 1 - RAW

        N_ACT = sum(not by_vector(p) for p in range(len(TILES)))
        N_DVE = len(TILES) - N_ACT
        UNITS = units()
        NU = len(UNITS)

        def r_bank(n):
            if 0 <= n - LAT_STD_AT < 4:
                return (0, 2, 1, 3)[n - LAT_STD_AT]
            return n % 2 + (4 if n in (0, 1, STD_AT[2], STD_AT[2] + 1) else 2)

        def first_unit(h, f):
            return 2 * h + f

        def pt_cols(u):
            kind, _, i = UNITS[u]
            return (i + 1) * P if kind == "mla" else SWA_GROUP * (P if i == 0 else 2 * P)

        block = ctx.enter_context(nc.Block())

        @block.sync
        def _(sp):
            def load_x(h):
                for q in range(2):
                    c = slice(q * KC // 2, (q + 1) * KC // 2)
                    sp.dma_start(x[:, c, half(h)], xT[:, c, half(h)]).then_inc(x_landed[2 * h + q], 16)

            def load_weights(n):
                if n >= RAW:
                    sp.wait_ge(*(first_lo_split, n - RAW + 1) if n < 2 * RAW else (lo_split, lo_count(n - RAW)))
                sp.dma_start(w_raw[:, n % RAW, :], wstream[n]).then_inc(raw_landed[n % RAW], 16)

            def load_modulation(n):
                if n >= 4:
                    sp.wait_ge(mod_used, n - 3)
                sp.dma_start(mod_raw[:, n % 4, :], w_modT[n]).then_inc(first_mod_landed[n % 4], 16)

            for n in range(4):
                load_modulation(n)
            load_x(0)
            for n in range(4, KC):
                load_modulation(n)
            for n in range(RAW):
                load_weights(n)
            load_x(1)
            for n in range(KC, KC + 4):
                load_modulation(n)
            load_weights(RAW)
            for n in range(KC + 4, GATE_AT):
                load_modulation(n)
            for n in range(RAW + 1, 2 * RAW):
                load_weights(n)
            with nc.sync.Fori(2, N_CHUNKS // RAW) as g:
                for j in range(RAW):
                    sp.wait_ge(lo_split, g * RAW + lo_count(j - RAW))
                    sp.dma_start(w_raw[:, j, :], wstream[bass.ds(g * RAW + j, 1), :, :].rearrange(
                        "a p d -> (a p) d")).then_inc(raw_landed[j], 16)
            for h in range(NH2):
                for c in range(0, KC, 2):
                    sp.wait_ge(out_ready, KC * h + c + 2)
                    sp.dma_start(out[:, c:c + 2, half(h)], x[:, c:c + 2, half(h)]).then_inc(out_saved, 16)
            sp.wait_ge(out_saved, 16 * KC)

        @block.gpsimd
        def _(pool):
            def sum_squares(s, h):
                for c in range(1, KC):
                    n = NORM_AT[s] + KC * h + c
                    pool.wait_ge(sq_done, n + 1)
                    if c == 1 and s > 0:
                        pool.wait_ge(sum_used, NH2 * (s - 1) + h + 1)
                    if c > 1:
                        pool.wait_ge(summed, (KC - 1) * (NH2 * s + h) + c - 1)
                    first = acc[:, h, :] if c > 1 else sq[:, (n - 1) % 2, :]
                    nc.gpsimd.tensor_tensor(acc[:, h, :], first, sq[:, n % 2, :], ALU.add
                                            ).then_inc(summed, 1)

            def load_modulation(n):
                if n < GATE_AT + 4:
                    pool.wait_ge(mod_used, n - 3)
                else:
                    pool.wait_ge(gate_summed, n - GATE_AT - 3)
                pool.dma_start(mod_raw[:, n % 4, :], w_modT[n]).then_inc(mod_landed[n % 4], 16)

            sum_squares(0, 0)
            for n in range(RAW):
                pool.wait_ge(hi_split, n + 1)
                nc.gpsimd.tensor_tensor(w_lo[:, n, :], w_raw[:, n, :], w_hi[:, n, :].bitcast(F32),
                                        ALU.subtract).then_inc(first_lo_split, 1)
            sum_squares(0, 1)
            pool.wait_ge(c_ready, 1)
            for n in range(GATE_AT, GATE_AT + 3):
                load_modulation(n)
            for n in range(GATE_AT, GATE_AT + KC):
                pool.wait_ge(mod_landed[n % 4], 16 * ((n - GATE_AT) // 4 + 1))
                nc.gpsimd.tensor_tensor(mod_raw[:, n % 4, :], mod_raw[:, n % 4, :], c_act[:], ALU.mult
                                        ).then_inc(gate_products, 1)
                load_modulation(n + 3)
            load_modulation(GATE_AT + KC + 3)
            with nc.gpsimd.Fori((GATE_AT + KC) // 4 + 1, MODC // 4) as g:
                for j in range(4):
                    pool.wait_ge(mod_used, g * 4 + (j - 3 - KC))
                    pool.dma_start(mod_raw[:, j, :], w_modT[bass.ds(g * 4 + j, 1), :, :].rearrange(
                        "a p d -> (a p) d")).then_inc(mod_landed[j], 16)
            pool.wait_ge(mod_used, MODC - KC)
            pool.dma_start(line[:], lm_in).then_inc(lm_landed, 16)
            pool.dma_start(onehot[:], oh_in).then_inc(oh_landed, 16)
            pool.dma_start(rel[:], rel_in).then_inc(rel_landed, 16)
            sum_squares(1, 0)
            sum_squares(1, 1)
            pool.dma_start(x_save, x[:]).then_inc(x_saved, 16)
            pool.wait_ge(x_saved, 16)
            pool.wait_ge(n_lo, LAT_AT)
            pool.dma_start(tab[:], tab_in).then_inc(tab_landed, 16)
            pool.wait_ge(tile_ready, 2 * N_IN)
            pool.wait_ge(line_saved, 16)
            pool.dma_start(bias[:], bass.AP(line_dram, P - 1, [[SWA_HEADS * LINE - 1, P], [LINE, SWA_HEADS],
                                                               [1, 2 * P]])).then_inc(bias_landed, 16)
            pool.wait_ge(tile_ready, len(TILES))
            pool.wait_ge(rope_done, NH2 * MLA_HEADS)
            pool.wait_ge(s_ready, WEIGHTS_AT[1])
            pool.dma_start(x[:], x_save).then_inc(x_back, 16)
            pool.wait_ge(x_back, 16)
            for s in (2, 3):
                for h in range(NH2):
                    sum_squares(s, h)

        @block.tensor
        def _(pe):
            def product(psum, wh, wl, ah, al, start, stop):
                pe.matmul(psum, wh, al, start=start, stop=False)
                pe.matmul(psum, wl, ah, start=False, stop=False)
                return pe.matmul(psum, wh, ah, start=False, stop=stop)

            def stats(first, tiles, bank):
                for k in range(tiles):
                    pe.wait_ge(sq_done, first + k + 1)
                    for b in range(HALF // P):
                        mm = pe.matmul(ps[:, bank, b:b + 1], sq[:, (first + k) % 2, blk(b)], ones[:, 0:1],
                                       start=(k == 0 and b == 0), stop=(k == tiles - 1),
                                       skip_group_check=True)
                    mm.then_inc(stat_done, 1)

            def total(s, h):
                pe.wait_ge(summed, (KC - 1) * (NH2 * s + h + 1))
                for b in range(HALF // P):
                    mm = pe.matmul(ps[:, r_bank(STD_AT[s] + h), b:b + 1], acc[:, h, blk(b)], ones[:, 0:1],
                                   start=(b == 0), stop=True, skip_group_check=True)
                mm.then_inc(sum_used, 1)

            def spread(n):
                pe.wait_ge(diag_done, n + 1)
                pe.matmul(ps[:, r_bank(n), :], ones, diag[:, n % 2, :], start=True, stop=True
                          ).then_inc(r_ready, 1)

            def row_product(z, slot, f, h, j, k):
                s = (W_FFN[z] + 2 * f + j) % SPLIT
                return product(ps[:, 2 * slot + j, :], w_hi[:, s, blk(k)], w_lo[:, s, blk(k)],
                               h_hi[:, k, half(h)], h_lo[:, k, half(h)], k == 0, k == KC - 1)

            def gate_up(z, i, f, h):
                n = 4 * ITERS * z + i * 4 + (2 * f + h)
                pe.wait_ge(uf_done, n - 1)
                for j in range(2):
                    if h == 0:
                        pe.wait_ge(lo_split, i * CPI + lo_count(W_FFN[z] + 2 * f + j))
                    for k in range(KC):
                        mm = row_product(z, h, f, h, j, k)
                mm.then_inc(gu_ready, 1)

            def first_units(z):
                s = 2 * z
                for h in range(NH2):
                    for t in range(KC + 2):
                        if h == 0 and t == 5:
                            total(s, 1)
                        if h == 0 and t == 6:
                            spread(STD_AT[s] + 1)
                        for f in range(FPI):
                            k = t - 2 * f
                            if not 0 <= k < KC:
                                continue
                            n = 4 * ITERS * z + first_unit(h, f)
                            if k == 0 and n >= 2:
                                pe.wait_ge(uf_done, n - 1)
                            if k == 0 and h == 0:
                                if z == 0:
                                    pe.wait_ge(first_lo_split, 2 + f)
                                if z == 1 or f == 1:
                                    pe.wait_ge(lo_split, lo_count(W_FFN[z] + 2 * f + 1))
                            if f == 0:
                                pe.wait_ge(n_lo, NORM_AT[s] + KC * h + k + 1)
                            for j in range(2):
                                mm = row_product(z, f, f, h, j, k)
                            if k == KC - 1:
                                mm.then_inc(gu_ready, 1)

            def down(z, i, h, d):
                n = X_AT[z] + i * 16 + (KC * h + d)
                if not isinstance(n, int) or n >= 4:
                    pe.wait_ge(x_added, n - 3)
                for f in range(FPI):
                    s = (W_FFN[z] + 2 * FPI + f) % SPLIT
                    mm = product(ps[:, 4 + d % 4, :], w_hi[:, s, blk(d)], w_lo[:, s, blk(d)],
                                 u_hi[:, f, half(h)], u_lo[:, f, half(h)], f == 0, f == FPI - 1)
                mm.then_inc(y_ready, 1)

            def ffn_step(z, i, first=False, last=False):
                if first:
                    first_units(z)
                else:
                    for f in range(FPI):
                        for h in range(NH2):
                            gate_up(z, i, f, h)
                pe.wait_ge(lo_split, i * CPI + lo_count(W_FFN[z] + CPI - 1))
                for h in range(NH2):
                    pe.wait_ge(u_lo_done, 4 * ITERS * z + i * 4 + (3 + h))
                    for d in range(KC):
                        down(z, i, h, d)
                        if last and h == 1 and d == 3:
                            total(2 * z + 1, 0)
                        if last and h == 1 and d == 5:
                            spread(STD_AT[2 * z + 1])
                if last and z == 1:
                    total(3, 1)

            def ffn(z):
                ffn_step(z, 0, first=True)
                with nc.tensor.Fori(1, ITERS - 1) as i:
                    ffn_step(z, i)
                ffn_step(z, ITERS - 1, last=True)

            def free_bank(p):
                if p >= 4:
                    vector, n = evacuated(p - 4)
                    pe.wait_ge(dve_emptied if vector else act_emptied, n)

            def in_product(m, h, k):
                s = (W_IN + m) % SPLIT
                return product(ps[:, 4 + TILES.index(("in", m, h)) % 4, :], w_hi[:, s, blk(k)],
                               w_lo[:, s, blk(k)], h_hi[:, k, half(h)], h_lo[:, k, half(h)],
                               k == 0, k == KC - 1)

            def first_projections():
                for h in range(NH2):
                    for t in range(KC + SIDE - 1):
                        if h == 0 and t == 5:
                            total(1, 1)
                        if h == 0 and t == 6:
                            spread(STD_AT[1] + 1)
                        for m in range(SIDE):
                            k = t - m
                            if not 0 <= k < KC:
                                continue
                            if k == 0:
                                pe.wait_ge(lo_split, lo_count(W_IN + m))
                                free_bank(SIDE * h + m)
                            if m == 0:
                                pe.wait_ge(n_lo, NORM_AT[1] + KC * h + k + 1)
                            mm = in_product(m, h, k)
                            if k == KC - 1:
                                mm.then_inc(tile_ready, 1)

            def mixer_in():
                first_projections()
                for m in range(SIDE, N_IN):
                    pe.wait_ge(lo_split, lo_count(W_IN + m))
                    for h in range(NH2):
                        p = 2 * m + h
                        free_bank(p)
                        for k in range(KC):
                            mm = in_product(m, h, k)
                        mm.then_inc(tile_ready, 1)
                        if p in (2 * VA, 2 * QA):
                            n = LAT_STD_AT + (0 if p == 2 * VA else 2)
                            spread(n)
                            spread(n + 1)
                    if m == KROPE:
                        stats(LAT_AT, 1, 0)
                        stats(LAT_AT + 1, 1, 2)
                        stats(LAT_AT + 2, 2, 1)
                        stats(LAT_AT + 4, 2, 3)
                    if m == QA:
                        pe.wait_ge(act_emptied, evacuated(2 * VA + 1)[1])
                        pe.wait_ge(t_done, LAT_AT + 4)
                        for b in range(NBLK):
                            tr = pe.transpose(ps[:, b // 4, blk(b % 4)], vT[:, blk(b)], ident)
                            if b % 4 == 3:
                                tr.then_inc(vt_ready, 1)

            def latent_products():
                s_kv = W_UKV % SPLIT
                s_q = [(W_UQ + k) % SPLIT for k in range(2)]
                pe.wait_ge(lo_split, lo_count(W_UKV))
                pe.wait_ge(n_lo, LAT_AT + 6)
                for p in range(MLA_FIRST, len(TILES)):
                    what, m, h = TILES[p]
                    free_bank(p)
                    out_p = ps[:, 4 + p % 4, :]
                    if what == "knope":
                        mm = product(out_p, w_hi[:, s_kv, blk(m)], w_lo[:, s_kv, blk(m)],
                                     kv_hi[:, half(h)], kv_lo[:, half(h)], True, True)
                    elif what == "v":
                        mm = product(out_p, kv_hi[:, blk(h)], kv_lo[:, blk(h)],
                                     w_hi[:, s_kv, HALF:D], w_lo[:, s_kv, HALF:D], True, True)
                    else:
                        col = {"qnope": m, "rope": MLA_HEADS + m}[what]
                        for k in range(2):
                            mm = product(out_p, w_hi[:, s_q[k], blk(col)], w_lo[:, s_q[k], blk(col)],
                                         q_hi[:, k, half(h)], q_lo[:, k, half(h)], k == 0, k == 1)
                    mm.then_inc(tile_ready, 1)

            def scores(u):
                kind, a, i = UNITS[u]
                if u >= 2:
                    if UNITS[u - 2][0] == "mla":
                        pe.wait_ge(exp_done, u - 1)
                    else:
                        pe.wait_ge(biased, sum(v[0] == "swa" for v in UNITS[:u - 1]))
                b0 = 2 * (u % 2)
                if kind == "mla":
                    parts = 1 if i == 0 else 2
                    w = (i + 1) * P // parts
                    for b in range(parts):
                        pe.matmul(ps[:, b0 + b, 0:w], o_all[:, 4 + a, blk(i)], k_nope[:, a, b * w:b * w + w],
                                  start=True, stop=False)
                    for b in range(parts):
                        r = slice(ROPE * b, ROPE * b + ROPE)
                        pe.matmul(ps[:, b0 + b, 0:w], q_r[r, a, blk(i)], k_r[r, b * w:b * w + w],
                                  start=False, stop=(b < parts - 1))
                    mm = pe.matmul(ps[:, b0 + parts - 1, w - P:w], ident_r[:], mask_r[:], start=False,
                                   stop=True)
                else:
                    lo, w = max(i - 1, 0) * P, P if i == 0 else 2 * P
                    for c in range(2):
                        for g in range(2):
                            rows = slice(SWA_DIM * g, SWA_DIM * g + SWA_DIM)
                            mm = pe.matmul(ps[:, b0 + g, c * w:c * w + w], o_all[rows, 2 * a + c, blk(i)],
                                           k_a[rows, lo:lo + w], start=True, stop=True)
                mm.then_inc(s_ready, 1)

            def turn(u):
                kind, _, i = UNITS[u]
                pe.wait_ge(p_done, u + 1)
                if u >= 1:
                    pe.wait_ge(pt_act, u)
                    pe.wait_ge(pt_dve, sum(pt_cols(v) > HALF for v in range(u)))
                if kind == "mla":
                    moves = [(j, j * P) for j in range(i + 1)]
                else:
                    kbs = 1 if i == 0 else 2
                    moves = [(kb * SWA_GROUP + c, (c * kbs + kb) * P)
                             for kb in range(kbs) for c in range(SWA_GROUP)]
                for j, lo in moves:
                    tr = pe.transpose(ps[:, 4 + j // 4, blk(j % 4)], p_sb[:, u % P_SLOTS, lo:lo + P], ident)
                tr.then_inc(pt_ready, 1)

            def values(u):
                kind, a, i = UNITS[u]
                pe.wait_ge(pt_act, u + 1)
                pe.wait_ge(pt_dve, sum(pt_cols(v) > HALF for v in range(u + 1)))
                if u >= 2:
                    pe.wait_ge(o_done, u - 1)
                if kind == "mla":
                    for j in range(i + 1):
                        mm = pe.matmul(ps[:, 6 + u % 2, 0:P], v_b[:, j, blk(a)], pt_sb[:, u % 2, blk(j)],
                                       start=(j == 0), stop=(j == i))
                else:
                    keys = [0] if i == 0 else [i - 1, i]
                    for n, b in enumerate(keys):
                        for g in range(2):
                            rows = slice(SWA_DIM * g, SWA_DIM * g + SWA_DIM)
                            lo = n * HALF + g * 2 * P
                            mm = pe.matmul(ps[rows, 6 + u % 2, 0:2 * P], v_a[:, b, rows],
                                           pt_sb[:, u % 2, lo:lo + 2 * P], start=(n == 0),
                                           stop=(n == len(keys) - 1))
                mm.then_inc(o_ready, 1)

            def attention():
                pe.wait_ge(act_emptied, N_ACT)
                pe.wait_ge(dve_emptied, N_DVE)
                pe.wait_ge(key_rotated, NH2)
                pe.wait_ge(rope_done, NH2 * MLA_HEADS)
                pe.wait_ge(va_done, 2)
                pe.wait_ge(mask_ready, 2)
                for u in range(NU + 3):
                    if u < NU:
                        scores(u)
                    if 2 <= u < NU + 2:
                        turn(u - 2)
                    if u >= 3:
                        values(u - 3)

            def mixer_out():
                for w, (d, h) in enumerate(OUT_TILES):
                    s = (W_OUT + d) % SPLIT
                    pe.wait_ge(lo_split, lo_count(W_OUT + d))
                    if w >= 4:
                        pe.wait_ge(x_added, X_MIX + w - 3)
                    last = w == len(OUT_TILES) - 1
                    if last:
                        total(2, 0)
                    for k in range(KC):
                        if d == 0:
                            pe.wait_ge(o_lo, KC * h + k + 1)
                        if last and k == 5:
                            spread(STD_AT[2])
                        mm = product(ps[:, 4 + w % 4, :], w_hi[:, s, blk(k)], w_lo[:, s, blk(k)],
                                     h_hi[:, k, half(h)], h_lo[:, k, half(h)], k == 0, k == KC - 1)
                    mm.then_inc(y_ready, 1)

            pe.wait_ge(const_landed, 16)
            total(0, 0)
            spread(0)
            ffn(0)
            pe.wait_ge(oh_landed, 16)
            pe.wait_ge(rel_landed, 16)
            pe.matmul(ps[0:SWA_HEADS, 0, 0:LINE], rel[:], onehot[:], start=True, stop=True
                      ).then_inc(line_ready, 1)
            mixer_in()
            latent_products()
            attention()
            mixer_out()
            ffn(1)
            spread(STD_AT[3] + 1)

        def squares_used(n):
            if LAT_AT <= n < NORM_AT[2]:
                return stat_done, n - LAT_AT + 1
            s = sum(n >= first for first in NORM_AT) - 1
            h, c = divmod(n - NORM_AT[s], KC)
            return summed, (KC - 1) * (NH2 * s + h) + max(c, 1)

        def chunk_free(n):
            m = n - W_IN
            if m < -2:
                return gu_ready, 4 * ITERS - (0 if m >= -4 else 2)
            if m < 0:
                return y_ready, X_MIX
            if m < N_IN:
                return tile_ready, TILES.index(("in", m, 1)) + 1
            if n < W_UKV:
                return tile_ready, len(TILES)
            if n == W_UKV:
                return tile_ready, TILES.index(("qnope", 0, 0))
            return y_ready, X_MIX + OUT_TILES.index((n - W_OUT, 1)) + 1

        @block.scalar
        def _(act):
            def hi_part(base, i, k, free):
                act.wait_ge(raw_landed[(base + k) % RAW], i * (16 * CPI // RAW) + 16 * ((base + k) // RAW + 1))
                if free is not None:
                    act.wait_ge(*free)
                act.activation(w_hi[:, (base + k) % SPLIT, :], w_raw[:, (base + k) % RAW, :], ACT.Copy
                               ).then_inc(hi_split, 1)

            def hi_of(n):
                hi_part(n, 0, 0, chunk_free(n - SPLIT))

            def square(n, source, ready):
                if ready is not None:
                    act.wait_ge(*ready)
                if n - 2 >= 0:
                    act.wait_ge(*squares_used(n - 2))
                act.activation(sq[:, n % 2, :], source, ACT.Square).then_inc(sq_done, 1)

            def deviation(n, size, sums):
                act.wait_ge(*sums)
                if n >= 4:
                    act.wait_ge(rstd_done, n - 3)
                act.activation(std[:, n % 4, :], ps[:, r_bank(n), 0:4], ACT.Sqrt, bias=eps[:, 0:1],
                               scale=1.0 / size).then_inc(std_done, 1)

            def shifted(s, h, c):
                n = NORM_AT[s] + KC * h + c
                act.wait_ge(t_done, n + 1)
                act.activation(h_hi[:, c, half(h)], tt[:, n % 2, :], ACT.Identity,
                               bias=mod[:, 3 * KC * s + 2 * c:3 * KC * s + 2 * c + 1]).then_inc(n_hi, 1)

            def norm(s, tile_at, between=lambda c: None):
                for c in range(KC):
                    square(NORM_AT[s] + c, x[:, c, half(0)], tile_at(0, c))
                lead = 2 if s in (1, 3) else 0
                for c in range(lead):
                    square(NORM_AT[s] + KC + c, x[:, c, half(1)], tile_at(1, c))
                deviation(STD_AT[s], D, (sum_used, NH2 * s + 1))
                if s == 0:
                    for k in range(RAW):
                        hi_part(k, 0, 0, None)
                for c in range(KC):
                    if s == 0 and c == KC - 2:
                        deviation(1, D, (sum_used, 2))
                    if s < 3:
                        shifted(s, 0, c)
                    for d in (c,) if s > 0 else range(6) if c == 3 else range(6, KC) if c == 4 else ():
                        if d >= lead:
                            square(NORM_AT[s] + KC + d, x[:, d, half(1)], tile_at(1, d))
                        if s == 0 and d == 2:
                            hi_part(RAW, 0, 0, None)
                if s > 0:
                    deviation(STD_AT[s] + 1, D, (sum_used, NH2 * s + 2))
                if s < 3:
                    for c in range(KC):
                        between(c)
                        shifted(s, 1, c)

            def sum_gate(n):
                act.wait_ge(gate_products, n + 1)
                act.activation(mod_raw[:, n % 4, :], mod_raw[:, n % 4, :], ACT.Copy,
                               accum_out=gate_acc[:, n:n + 1]).then_inc(gate_summed, 1)

            def first_units(z):
                def between(c):
                    if c == (4 if z == 0 else 3):
                        silu(z, 0, 0, 0, first_unit(0, 0))
                        u_hi_part(z, 0, 0, 0, first_unit(0, 0))
                    if c == (6 if z == 0 else 5):
                        silu(z, 0, 1, 0, first_unit(0, 1))
                        u_hi_part(z, 0, 1, 0, first_unit(0, 1))
                    if z == 0 and c % 2 == 1:
                        sum_gate(c // 2)
                return between

            def silu(z, i, f, h, unit=None):
                unit = 2 * f + h if unit is None else unit
                n = 4 * ITERS * z + i * 4 + unit
                act.wait_ge(gu_ready, n + 1)
                if not isinstance(n, int) or n >= 2:
                    act.wait_ge(uf_done, n - 1)
                act.activation(sil[:, unit % 2, :], ps[:, 2 * (unit % 2), :], ACT.Silu).then_inc(sil_done, 1)

            def u_hi_part(z, i, f, h, unit=None):
                unit = 2 * f + h if unit is None else unit
                act.wait_ge(uf_done, 4 * ITERS * z + i * 4 + (unit + 1))
                act.activation(u_hi[:, f, half(h)], uf[:, unit % 2, :], ACT.Copy).then_inc(u_hi_done, 1)

            def first_step(z):
                w = W_FFN[z]
                for k in (4, 5):
                    hi_part(w, 0, k, chunk_free(w + k - SPLIT) if z == 1 else None)
                if z == 0:
                    for n in range(4, 7):
                        sum_gate(n)
                for f in range(FPI):
                    silu(z, 0, f, 1, first_unit(1, f))
                    u_hi_part(z, 0, f, 1, first_unit(1, f))
                    if z == 0 and f == 0:
                        sum_gate(7)
                    for k in (2 * f, 2 * f + 1):
                        hi_part(w + CPI, 0, k, (gu_ready, 4 * ITERS * z + first_unit(1, f) + 1))

            def ffn_step(z, i, last=False):
                w = W_FFN[z]
                after = 4 * ITERS * z + i * 4
                silu(z, i, 0, 0)
                u_hi_part(z, i, 0, 0)
                for k in (4, 5):
                    hi_part(w, i, k, (y_ready, X_AT[z] + i * 16))
                silu(z, i, 0, 1)
                u_hi_part(z, i, 0, 1)
                more = not (last and z == 1)
                for k in (0, 1) if more else ():
                    hi_part(w + CPI, i, k, (gu_ready, after + 2))
                silu(z, i, 1, 0)
                u_hi_part(z, i, 1, 0)
                silu(z, i, 1, 1)
                u_hi_part(z, i, 1, 1)
                for k in (2, 3) if more else ():
                    hi_part(w + CPI, i, k, (gu_ready, after + 4))

            def ffn(z):
                first_step(z)
                with nc.scalar.Fori(1, ITERS - 1) as i:
                    ffn_step(z, i)
                ffn_step(z, ITERS - 1, last=True)
                tile = X_AT[z] + 16 * (ITERS - 1)

                def between(c):
                    if c < SIDE:
                        empty(c)

                norm(2 * z + 1, lambda h, c: (x_added, tile + KC * h + c + 1), between)

            def empty(p):
                what, m, h = TILES[p]
                if by_vector(p):
                    return
                if what == "in":
                    to = {KV: kvl[:, half(h)], Q0: ql[:, 0, half(h)], Q1: ql[:, 1, half(h)],
                          KA: k_a[:, half(h)], VA: vT[:, half(h)]}.get(m)
                    if to is None:
                        to = o_all[:, m - QA, half(h)]
                elif what == "knope":
                    to = k_nope[:, m, half(h)]
                elif what == "v":
                    to = v_b[:, h, :]
                else:
                    to = o_all[:, 4 + m, half(h)]
                act.wait_ge(tile_ready, p + 1)
                act.activation(to, ps[:, 4 + p % 4, :], ACT.Copy).then_inc(act_emptied, 1)

            def latent_square(v):
                source = (kvl[:, half(v)] if v < 2 else ql[:, v % 2, half((v - 2) // 2)])
                square(LAT_AT + v, source, (act_emptied, evacuated(TILES.index(("in", Q1, 1)))[1]))

            def latent_hi(v):
                to = kv_hi[:, half(v)] if v < 2 else q_hi[:, v % 2, half((v - 2) // 2)]
                if v == 0:
                    act.wait_ge(x_saved, 16)
                act.wait_ge(t_done, LAT_AT + v + 1)
                act.activation(to, tt[:, (LAT_AT + v) % 2, :], ACT.Copy).then_inc(n_hi, 1)

            def mixer_in():
                hi_of(W_IN + 4)
                hi_of(W_IN + 5)
                for m in range(SIDE):
                    empty(SIDE + m)
                    if m > 0:
                        hi_of(W_IN + m + 5)
                latent_square(0)
                latent_square(1)
                act.wait_ge(line_added, 1)
                act.dma_start(line_dram.ap().rearrange("q h t -> h q t"), line[:].rearrange(
                    "h (q t) -> h q t", q=1).broadcast_to([SWA_HEADS, P, LINE])).then_inc(line_saved, 16)
                for m in range(SIDE, N_IN):
                    empty(2 * m)
                    hi_of(W_IN + m + 5)
                    empty(2 * m + 1)
                    if m == KROPE:
                        for v in range(2, 6):
                            latent_square(v)
                        for j, (tiles, size) in enumerate(
                                [(1, KV_RANK), (2, KV_RANK), (4, Q_RANK), (6, Q_RANK)]):
                            deviation(LAT_STD_AT + j, size, (stat_done, tiles))
                    if VA <= m <= VA + 2:
                        latent_hi(2 * (m - VA))
                        latent_hi(2 * (m - VA) + 1)
                    if m == QA:
                        act.wait_ge(line_saved, 16)
                        for j in range(2):
                            act.wait_ge(vt_ready, j + 1)
                            act.activation(v_a[:, 4 * j:4 * j + 4, :], ps[:, j, :].rearrange(
                                "p (b d) -> p b d", b=4), ACT.Copy).then_inc(va_done, 1)

            def exps(u):
                kind, a, i = UNITS[u]
                s = u % 2
                act.wait_ge(max_done, u + 1)
                p_u = p_sb[:, u % P_SLOTS, :]
                if kind == "mla":
                    if u >= P_SLOTS:
                        act.wait_ge(pt_ready, u - P_SLOTS + 1)
                    w = (i + 1) * P
                    parts = 1 if i == 0 else 2
                    act.activation(p_u[:, 0:w].rearrange("p (b c) -> p b c", b=parts),
                                   ps[:, 2 * s:2 * s + parts, 0:w // parts], ACT.Exp,
                                   bias=negm[:, s, 0:1], scale=MLA_SCALE,
                                   accum_out=den[:, s, 0:1]).then_inc(exp_done, 1)
                else:
                    w = P if i == 0 else 2 * P
                    for c in range(SWA_GROUP):
                        act.activation(p_u[:, c * w:(c + 1) * w], p_u[:, c * w:(c + 1) * w], ACT.Exp,
                                       bias=negm[:, s, c:c + 1], accum_out=den[:, s, c:c + 1])
                    act.activation(esink[:, s, :], dsink[:, s, :], ACT.Exp).then_inc(exp_done, 1)

            def copy_turned(u):
                act.wait_ge(pt_ready, u + 1)
                if u >= 2:
                    act.wait_ge(o_ready, u - 1)
                w = min(pt_cols(u), HALF)
                act.activation(pt_sb[:, u % 2, 0:w], ps[:, 4, 0:w], ACT.Copy).then_inc(pt_act, 1)

            def copy_output(u):
                kind, a, i = UNITS[u]
                act.wait_ge(o_ready, u + 1)
                if kind == "mla":
                    act.activation(o_all[:, 4 + a, blk(i)], ps[:, 6 + u % 2, 0:P], ACT.Copy).then_inc(o_done, 1)
                else:
                    act.activation(o_all[:, 2 * a:2 * a + 2, blk(i)],
                                   ps[:, 6 + u % 2, 0:2 * P].rearrange("p (c q) -> p c q", c=2),
                                   ACT.Copy).then_inc(o_done, 1)

            def attention():
                for u in range(NU + 3):
                    if 2 <= u < NU + 2:
                        copy_turned(u - 2)
                    if u < NU:
                        exps(u)
                    if u in WEIGHTS_AT:
                        hi_of(W_OUT + 3 + WEIGHTS_AT.index(u))
                    if u >= 3:
                        copy_output(u - 3)

            def mixer_out():
                act.wait_ge(o_done, NU)
                for h in range(NH2):
                    for c in range(KC):
                        act.activation(h_hi[:, c, half(h)], o_all[:, c, half(h)], ACT.Copy).then_inc(o_hi, 1)
                for d in range(1, 7):
                    hi_of(W_OUT + d + 5)

            act.dma_start(c_act[:], c_in).then_inc(c_landed, 16)
            act.dma_start(small[:], small_in).then_inc(small_landed, 16)
            act.dma_start(consts[:], const_in).then_inc(const_landed, 16)
            act.dma_start(sinks[:], sinks_in).then_inc(sinks_landed, 16)
            act.wait_ge(c_landed, 16)
            act.activation(c_act[:], c_act[:], ACT.Silu).then_inc(c_ready, 1)
            act.wait_ge(eps_ready, 1)
            norm(0, lambda h, c: (x_landed[2 * h + c // (KC // 2)], 16), first_units(0))
            ffn(0)
            mixer_in()
            for p in range(MLA_FIRST, len(TILES)):
                empty(p)
                if TILES[p] == ("qnope", 1, 0):
                    hi_of(W_OUT + 2)
                    act.wait_ge(rope_done, NH2 * MLA_HEADS)
                    act.activation(ident_r[:], ident, ACT.Copy).then_inc(mask_ready, 1)
                    act.activation(mask_r[:], mask, ACT.Copy).then_inc(mask_ready, 1)
            attention()
            mixer_out()
            norm(2, lambda h, c: (x_added, X_MIX + OUT_TILES.index((c, h)) + 1), first_units(1))
            ffn(1)

        @block.vector
        def _(dve):
            count = {}

            def step(ins, signal):
                count[signal.name] = count.get(signal.name, 0) + 1
                ins.then_inc(signal, 1)
                dve.wait_ge(signal, count[signal.name])

            def modulation(j):
                done = j - KC // 4 if not isinstance(j, int) or 4 * j > GATE_AT else j
                for k in range(4):
                    if isinstance(j, int) and 4 * j < GATE_AT:
                        dve.wait_ge(first_mod_landed[k], j * 16 + 16)
                    else:
                        dve.wait_ge(mod_landed[k], j * 16 + (16 - 4 * GATE_AT))
                    if not isinstance(j, int) or j > 0:
                        dve.wait_ge(mod_ready, done)
                    dve.tensor_tensor_reduce(out=mod_raw[:, k, :], in0=mod_raw[:, k, :], in1=c_act[:],
                                             scale=1.0, scalar=0.0, op0=ALU.mult, op1=ALU.add,
                                             accum_out=mod_acc[:, k:k + 1]).then_inc(mod_used, 1)
                dve.wait_ge(mod_used, done * 4 + 4)
                dve.tensor_tensor(mod[:, bass.ds(j * 4, 4)], mod_acc[:], small[:, bass.ds(j * 4, 4)],
                                  ALU.add).then_inc(mod_ready, 1)

            def shift(s, c):
                n = 3 * KC * s + 2 * c
                return mod[:, n:n + 1]

            def scale_vector(s, c, n):
                group = 6 * s + (2 * (c + n) + 3) // 4 - (2 if s > 0 else 0)
                dve.wait_ge(mod_ready, group)
                c0 = 3 * KC * s + 2 * c
                scale = mod[:, c0:c0 + 2 * n].rearrange("p (c t) -> p c t", t=2)[:, :, 1]
                dve.scalar_tensor_tensor(out=scale_v[:, s, c:c + n], in0=scale, scalar=1.0,
                                         in1=gain(s)[:, c:c + n], op0=ALU.add, op1=ALU.mult
                                         ).then_inc(vec_ready, 1)

            def gate_vector(s):
                c0 = 3 * KC * s + 2 * KC
                if s == 0:
                    dve.wait_ge(gate_summed, KC)
                    step(dve.tensor_tensor(gate_acc[:], gate_acc[:], bmod[:, c0:c0 + KC], ALU.add),
                         gate_biased)
                    source = gate_acc[:]
                else:
                    dve.wait_ge(mod_ready, 6 * s + 4)
                    source = mod[:, c0:c0 + KC]
                dve.tensor_scalar(gate_v[:, s, :], source, 1.0 if s == 1 else 0.5, None,
                                  ALU.mult).then_inc(vec_ready, 1)

            def lo_part(base, i, k):
                dve.wait_ge(hi_split, i * CPI + (base + k + 1))
                s = (base + k) % SPLIT
                dve.tensor_tensor(w_lo[:, s, :], w_raw[:, (base + k) % RAW, :], w_hi[:, s, :].bitcast(F32),
                                  ALU.subtract).then_inc(lo_split, 1)

            def lo_of(n):
                lo_part(n, 0, 0)

            def invert(n):
                dve.wait_ge(std_done, n + 1)
                dve.reciprocal(rstd[:, n % 4, :], std[:, n % 4, :]).then_inc(rstd_done, 1)
                dve.wait_ge(rstd_done, n + 1)
                if n >= 2:
                    dve.wait_ge(r_ready, n - 1)
                dve.tensor_tensor(diag[:, n % 2, :].rearrange("p (b t) -> p b t", b=4),
                                  ident.rearrange("p (b t) -> p b t", b=1).broadcast_to([P, 4, P]),
                                  rstd[:, n % 4, :].rearrange("p (b t) -> p b t", t=1).broadcast_to([P, 4, P]),
                                  ALU.mult).then_inc(diag_done, 1)

            def scaled(n, source, scale, r):
                dve.wait_ge(r_ready, r + 1)
                if n >= 2:
                    dve.wait_ge(n_lo, n - 1)
                dve.scalar_tensor_tensor(out=tt[:, n % 2, :], in0=source, scalar=scale, in1=ps[:, r_bank(r), :],
                                         op0=ALU.mult, op1=ALU.mult).then_inc(t_done, 1)

            def shifted_lo(s, h, c):
                n = NORM_AT[s] + KC * h + c
                dve.wait_ge(n_hi, n + 1)
                dve.scalar_tensor_tensor(out=h_lo[:, c, half(h)], in0=tt[:, n % 2, :],
                                         scalar=shift(s, c),
                                         in1=h_hi[:, c, half(h)].bitcast(F32), op0=ALU.add,
                                         op1=ALU.subtract).then_inc(n_lo, 1)

            def scaled_tile(s, h, c):
                scaled(NORM_AT[s] + KC * h + c, x[:, c, half(h)], scale_v[:, s, c:c + 1], STD_AT[s] + h)

            def first_norm():
                modulation(0)
                modulation(1)
                invert(0)
                for n, (c0, width) in enumerate([(0, 4), (4, 2), (6, 2)]):
                    if n > 0:
                        modulation(n + 1)
                    if n == 1:
                        lo_of(RAW)
                    scale_vector(0, c0, width)
                    if n == 2:
                        invert(1)
                    dve.wait_ge(vec_ready, n + 1)
                    for c in range(c0, c0 + width + 1):
                        if c < c0 + width:
                            scaled_tile(0, 0, c)
                        if c > c0:
                            shifted_lo(0, 0, c - 1)

            def norm_half(s, h, between=lambda c: None):
                for c in range(KC + 1):
                    between(c)
                    if c < KC:
                        scaled_tile(s, h, c)
                    if c >= 1:
                        shifted_lo(s, h, c - 1)
                if h == 0:
                    invert(STD_AT[s] + 1)

            def final_half(h, between=lambda c: None):
                dve.wait_ge(r_ready, STD_AT[3] + h + 1)
                for c in range(KC):
                    dve.scalar_tensor_tensor(out=x[:, c, half(h)], in0=x[:, c, half(h)],
                                             scalar=gain(3)[:, c:c + 1], in1=ps[:, r_bank(STD_AT[3] + h), :],
                                             op0=ALU.mult, op1=ALU.mult).then_inc(out_ready, 1)
                    between(c)

            def multiply(z, i, f, h, unit=None):
                unit = 2 * f + h if unit is None else unit
                n = 4 * ITERS * z + i * 4 + unit
                slot = unit % 2
                dve.wait_ge(sil_done, n + 1)
                if not isinstance(n, int) or n >= 2:
                    dve.wait_ge(u_lo_done, n - 1)
                dve.tensor_tensor(uf[:, slot, :], sil[:, slot, :], ps[:, 2 * slot + 1, :], ALU.mult
                                  ).then_inc(uf_done, 1)
                dve.wait_ge(u_hi_done, n + 1)
                dve.tensor_tensor(u_lo[:, f, half(h)], uf[:, slot, :], u_hi[:, f, half(h)].bitcast(F32),
                                  ALU.subtract).then_inc(u_lo_done, 1)

            def first_units(z):
                def between(c):
                    if c == (4 if z == 0 else 3):
                        multiply(z, 0, 0, 0, first_unit(0, 0))
                    if c == (6 if z == 0 else 5):
                        multiply(z, 0, 1, 0, first_unit(0, 1))
                return between

            def add(n, bank, d, h, s):
                dve.wait_ge(y_ready, n + 1)
                dve.scalar_tensor_tensor(out=x[:, d, half(h)], in0=ps[:, bank, :], scalar=gate_v[:, s, d:d + 1],
                                         in1=x[:, d, half(h)], op0=ALU.mult, op1=ALU.add).then_inc(x_added, 1)

            def ffn_step(z, i, first=False, last=False):
                w = W_FFN[z]
                more = not (last and z == 1)
                if first:
                    for k in (4, 5):
                        lo_part(w, i, k)
                    for f in range(FPI):
                        multiply(z, i, f, 1, first_unit(1, f))
                        if f == 0:
                            for k in (0, 1):
                                lo_part(w + CPI, i, k)
                    if z == 0:
                        gate_vector(0)
                        dve.wait_ge(vec_ready, 4)
                else:
                    multiply(z, i, 0, 0)
                    for k in (4, 5):
                        lo_part(w, i, k)
                    if z == 0:
                        modulation(i + 5)
                    multiply(z, i, 0, 1)
                    if z == 0 and last:
                        for j in (MODC // 4 - 2, MODC // 4 - 1):
                            modulation(j)
                        for s in (1, 2):
                            scale_vector(s, 0, KC)
                            gate_vector(s)
                        dve.wait_ge(vec_ready, 8)
                    for k in (0, 1) if more else ():
                        lo_part(w + CPI, i, k)
                    multiply(z, i, 1, 0)
                    multiply(z, i, 1, 1)

                def added(h, d):
                    add(X_AT[z] + i * 16 + (KC * h + d), 4 + d % 4, d, h, 2 * z)

                for d in range(KC):
                    added(0, d)
                    if d in (1, 3) and more:
                        lo_part(w + CPI, i, 2 + d // 2)
                if not last:
                    for d in range(KC):
                        added(1, d)
                    return
                for d in range(6):
                    added(1, d)
                    if d == 4:
                        invert(STD_AT[2 * z + 1])

                def between(c):
                    if 1 <= c <= 2:
                        added(1, 5 + c)

                if z == 0:
                    norm_half(1, 0, between)
                    norm_half(1, 1)
                else:
                    final_half(0, between)
                    invert(STD_AT[3] + 1)
                    final_half(1)

            def ffn(z):
                ffn_step(z, 0, first=True)
                with nc.vector.Fori(1, ITERS - 1) as i:
                    ffn_step(z, i)
                ffn_step(z, ITERS - 1, last=True)

            def rotate(p, to, done):
                bank = ps[:, 4 + p % 4, :]
                h = TILES[p][2]
                dve.wait_ge(tile_ready, p + 1)
                r = slice(0, ROPE)
                dve.tensor_tensor(tt[r, 0, :], bank[r, :], tab[r, 0, half(h)], ALU.mult)
                ins = dve.tensor_tensor(tt[r, 1, :], bank[ROPE:P, :], tab[ROPE:P, 1, half(h)], ALU.mult)
                ins.then_inc(dve_emptied, 1)
                dve.wait_ge(dve_emptied, evacuated(p)[1])
                dve.tensor_tensor(to[r, :], tt[r, 0, :], tt[r, 1, :], ALU.add)
                step(dve.tensor_tensor(to[ROPE:P, :], tt[r, 0, :], tt[r, 1, :], ALU.add), done)

            def latent(v):
                h = v if v < 2 else (v - 2) // 2
                source = kvl[:, half(h)] if v < 2 else ql[:, v % 2, half(h)]
                g = lat_gain[:, 2:3] if v < 2 else lat_gain[:, v % 2:v % 2 + 1]
                r = LAT_STD_AT + (h if v < 2 else 2 + h)
                scaled(LAT_AT + v, source, g, r)

            def latent_lo(v):
                h = v if v < 2 else (v - 2) // 2
                hi, lo = (kv_hi[:, half(h)], kv_lo[:, half(h)]) if v < 2 else (
                    q_hi[:, v % 2, half(h)], q_lo[:, v % 2, half(h)])
                dve.wait_ge(n_hi, LAT_AT + v + 1)
                dve.tensor_tensor(lo, tt[:, (LAT_AT + v) % 2, :], hi.bitcast(F32), ALU.subtract
                                  ).then_inc(n_lo, 1)

            def mixer_in():
                dve.wait_ge(line_ready, 1)
                dve.wait_ge(lm_landed, 16)
                dve.tensor_tensor(line[:], ps[0:SWA_HEADS, 0, 0:LINE], line[:], ALU.add
                                  ).then_inc(line_added, 1)
                for n in range(W_IN + 4, W_IN + 9):
                    lo_of(n)
                for m in range(SIDE, N_IN):
                    lo_of(W_IN + m + 5)
                    if m == KROPE:
                        dve.wait_ge(tab_landed, 16)
                        for h in range(NH2):
                            rotate(2 * KROPE + h, k_r[:, half(h)], key_rotated)
                        invert(LAT_STD_AT)
                        invert(LAT_STD_AT + 1)
                    if m == VA:
                        latent(0)
                        latent(1)
                        invert(LAT_STD_AT + 2)
                        invert(LAT_STD_AT + 3)
                    if VA <= m <= VA + 2:
                        v = 2 * (m - VA)
                        latent_lo(v)
                        latent_lo(v + 1)
                        if v < 4:
                            latent(v + 2)
                            latent(v + 3)

            def latent_products():
                for p in range(MLA_FIRST, len(TILES)):
                    what, m, h = TILES[p]
                    if what == "rope":
                        rotate(p, q_r[:, m, half(h)], rope_done)
                lo_of(W_OUT + 2)

            def maxima(u):
                kind, a, i = UNITS[u]
                s = u % 2
                dve.wait_ge(s_ready, u + 1)
                if kind == "mla":
                    parts = 1 if i == 0 else 2
                    step(dve.tensor_reduce(mx[:, s, 0:1], ps[:, 2 * s:2 * s + parts, 0:(i + 1) * P // parts],
                                           AX.XY, ALU.max), max_part)
                    dve.tensor_scalar(negm[:, s, 0:1], mx[:, s, 0:1], -MLA_SCALE, None, ALU.mult
                                      ).then_inc(max_done, 1)
                    return
                w = P if i == 0 else 2 * P
                if u >= P_SLOTS:
                    dve.wait_ge(pt_ready, u - P_SLOTS + 1)
                heads = slice(SWA_GROUP * a, SWA_GROUP * a + SWA_GROUP)
                p4 = p_sb[:, u % P_SLOTS, 0:SWA_GROUP * w].rearrange("p (c k) -> p c k", c=SWA_GROUP)
                for g in range(2):
                    ins = dve.scalar_tensor_tensor(
                        out=p4[:, 2 * g:2 * g + 2, :], in0=ps[:, 2 * s + g, 0:2 * w].rearrange(
                            "p (c k) -> p c k", c=2), scalar=SWA_SCALE,
                        in1=bias[:, SWA_GROUP * a + 2 * g:SWA_GROUP * a + 2 * g + 2, 2 * P - w:2 * P],
                        op0=ALU.mult, op1=ALU.add)
                step(ins, biased)
                step(dve.tensor_reduce(mx[:, s, :], p4, AX.X, ALU.max), max_part)
                step(dve.tensor_tensor(mx[:, s, :], mx[:, s, :], sinks[:, heads], ALU.max), max_part)
                dve.tensor_scalar(negm[:, s, :], mx[:, s, :], -1.0, None, ALU.mult)
                dve.tensor_tensor(dsink[:, s, :], sinks[:, heads], mx[:, s, :], ALU.subtract
                                  ).then_inc(max_done, 1)

            def normalise(u):
                kind, a, i = UNITS[u]
                s = u % 2
                p_u = p_sb[:, u % P_SLOTS, :]
                dve.wait_ge(exp_done, u + 1)
                if kind == "mla":
                    w = (i + 1) * P
                    step(dve.reciprocal(rden[:, s, 0:1], den[:, s, 0:1]), den_part)
                    dve.tensor_scalar(p_u[:, 0:w], p_u[:, 0:w], rden[:, s, 0:1], None, ALU.mult
                                      ).then_inc(p_done, 1)
                    return
                w = P if i == 0 else 2 * P
                step(dve.tensor_tensor(den[:, s, :], den[:, s, :], esink[:, s, :], ALU.add), den_part)
                step(dve.reciprocal(rden[:, s, :], den[:, s, :]), den_part)
                for c in range(SWA_GROUP):
                    ins = dve.tensor_scalar(p_u[:, c * w:(c + 1) * w], p_u[:, c * w:(c + 1) * w],
                                            rden[:, s, c:c + 1], None, ALU.mult)
                ins.then_inc(p_done, 1)

            def copy_turned(u):
                w = pt_cols(u) - HALF
                if w <= 0:
                    return
                dve.wait_ge(pt_ready, u + 1)
                if u >= 2:
                    dve.wait_ge(o_ready, u - 1)
                dve.tensor_copy(pt_sb[:, u % 2, HALF:HALF + w], ps[:, 5, 0:w]).then_inc(pt_dve, 1)

            def attention():
                dve.wait_ge(sinks_landed, 16)
                dve.wait_ge(bias_landed, 16)
                for u in range(NU + 2):
                    if u < NU:
                        maxima(u)
                    if u >= 2:
                        copy_turned(u - 2)
                    if 1 <= u <= NU:
                        normalise(u - 1)
                    if u - 1 in WEIGHTS_AT:
                        lo_of(W_OUT + 3 + WEIGHTS_AT.index(u - 1))

            def mixer_out():
                for h in range(NH2):
                    for c in range(KC):
                        dve.wait_ge(o_hi, KC * h + c + 1)
                        dve.tensor_tensor(h_lo[:, c, half(h)], o_all[:, c, half(h)],
                                          h_hi[:, c, half(h)].bitcast(F32), ALU.subtract).then_inc(o_lo, 1)
                dve.wait_ge(x_back, 16)
                for w, (d, h) in enumerate(OUT_TILES):
                    if w == len(OUT_TILES) - 1:
                        invert(STD_AT[2])
                        return
                    add(X_MIX + w, 4 + w % 4, d, h, 1)
                    for n in range(W_OUT + SPLIT, W_FFN[1] + 4):
                        if OUT_TILES.index((n - SPLIT - W_OUT, 1)) == w:
                            lo_of(n)

            def last_output(c):
                w = len(OUT_TILES) - 1
                d, h = OUT_TILES[w]
                if c == 3:
                    add(X_MIX + w, 4 + w % 4, d, h, 1)

            dve.memset(eps[:], EPS).then_inc(eps_ready, 1)
            dve.wait_ge(small_landed, 16)
            dve.wait_ge(c_ready, 1)
            first_norm()
            norm_half(0, 1, first_units(0))
            ffn(0)
            mixer_in()
            latent_products()
            attention()
            mixer_out()
            norm_half(2, 0, last_output)
            norm_half(2, 1, first_units(1))
            ffn(1)


def _columns(w, cols):
    return w[:, cols].reshape(-1, P, P).transpose(1, 0, 2).reshape(P, -1)


def weight_stream(np, gate1, up1, down1, w_in, w_uq, w_ukv, w_o, gate2, up2, down2):
    chunks = []

    def ffn(gate, up, down):
        for i in range(ITERS):
            fs = [slice((FPI * i + f) * P, (FPI * i + f + 1) * P) for f in range(FPI)]
            for f in fs:
                chunks.append(_columns(gate, f))
                chunks.append(_columns(up, f))
            for f in fs:
                chunks.append(down[f, :])

    ffn(gate1, up1, down1)
    r = np.arange
    q_at, k_at, v_at, ql_at, kv_at, kr_at = 0, 512, 640, 768, 1024, 1152
    rope = r(kr_at, kr_at + ROPE)
    swapped = np.concatenate([rope[ROPE // 2:], rope[:ROPE // 2]])
    for cols in ([r(kv_at, kv_at + P), r(ql_at, ql_at + P), r(ql_at + P, ql_at + 2 * P),
                  r(k_at, k_at + P), np.concatenate([rope, swapped]), r(v_at, v_at + P)]
                 + [np.concatenate([r(q_at + 64 * c, q_at + 64 * c + 64),
                                    r(q_at + 256 + 64 * c, q_at + 256 + 64 * c + 64)]) for c in range(4)]):
        chunks.append(_columns(w_in, cols))
    hd = NOPE + ROPE
    nope = np.concatenate([r(h * hd, h * hd + NOPE) for h in range(MLA_HEADS)])
    rope = [r(h * hd + NOPE, (h + 1) * hd) for h in range(MLA_HEADS)]
    rope = [np.concatenate([c, c[ROPE // 2:], c[:ROPE // 2]]) for c in rope]
    cols = np.concatenate([nope, *rope])
    for k in range(2):
        chunks.append(w_uq[k * P:(k + 1) * P, cols])
    chunks.append(w_ukv[:, np.concatenate([r(h * 256 + o, h * 256 + o + P) for o in (0, P)
                                           for h in range(MLA_HEADS)])])
    rows = np.concatenate([np.concatenate([r(64 * c, 64 * c + 64), r(256 + 64 * c, 256 + 64 * c + 64)])
                           for c in range(4)] + [r(512, 1024)])
    for d in range(KC):
        chunks.append(_columns(w_o[rows, :], slice(d * P, (d + 1) * P)))
    ffn(gate2, up2, down2)
    return np.stack(chunks)


def shape_constants(np):
    f = np.float32
    causal = np.where(np.arange(P)[None, :] > np.arange(P)[:, None], f(-1e30), f(0))
    consts = np.stack([np.eye(P, dtype=f), causal.astype(f), np.ones((P, P), f)], axis=1)
    inv = np.power(f(10000.0), -np.arange(0, ROPE, 2, dtype=f) / f(ROPE)).astype(f)
    ang = (np.arange(T, dtype=f)[:, None] * inv[None, :]).astype(f)
    cos, sin = np.cos(ang).T.astype(f), np.sin(ang).T.astype(f)
    tab = np.stack([np.concatenate([cos, cos, cos, cos]), np.concatenate([-sin, sin, -sin, sin])], axis=1)
    dist = 2 * P - 1 - np.arange(LINE)
    ok = (dist >= 0) & (dist < P)
    n = np.maximum(dist, 0)
    large = 16 + (np.log(np.maximum(n, 1).astype(f) / f(16)) / f(np.log(8.0)) * f(16)).astype(np.int32)
    bucket = np.where(n < 16, n, np.minimum(large, BUCKETS - 1))
    onehot = ((bucket[None, :] == np.arange(BUCKETS)[:, None]) & ok[None, :]).astype(f)
    linemask = np.broadcast_to(np.where(ok, f(0), f(-1e30)), (SWA_HEADS, LINE)).astype(f)
    return consts, tab, onehot, linemask


def kernel(x, c, w_mod, b_mod, norm_ffn1, ffn1_gate, ffn1_up, ffn1_down, norm_mix, w_in, q_norm, kv_norm,
           w_uq, w_ukv, sinks, w_o, norm_ffn2, ffn2_gate, ffn2_up, ffn2_down, rel_bias, norm_final):
    import numpy as np
    import concourse.bacc as bacc
    from concourse.bass_utils import run_bass_kernel_spmd

    def a(v):
        return np.asarray(v)

    def by_partition(v):
        return a(v).reshape(-1, P).T

    mod_order = [3 * KC * s + n for s in range(3)
                 for n in [j * KC + c for c in range(KC) for j in range(2)] + list(range(2 * KC, 3 * KC))]

    consts, tab, onehot, linemask = shape_constants(np)
    heads = [0, 1, 4, 5, 2, 3, 6, 7]
    arrays = {
        "xT_in": a(x)[0].T.reshape(KC, P, T).transpose(1, 0, 2),
        "c_in": np.broadcast_to(a(c)[0], (P, D)),
        "w_modT_in": a(w_mod)[0].T.reshape(MODC, P, D)[mod_order],
        "small_in": np.concatenate([by_partition(v) for v in (
            a(b_mod)[0].reshape(MODC, P)[mod_order], a(norm_ffn1)[0], a(norm_mix)[0], a(norm_ffn2)[0],
            a(norm_final), a(q_norm)[0],
            a(kv_norm)[0])], axis=1),
        "wstream_in": weight_stream(np, *(a(w)[0] for w in (
            ffn1_gate, ffn1_up, ffn1_down, w_in, w_uq, w_ukv, w_o, ffn2_gate, ffn2_up, ffn2_down))),
        "const_in": consts,
        "tab_in": tab,
        "sinks_in": np.broadcast_to(a(sinks)[0][heads], (P, SWA_HEADS)),
        "rel_in": a(rel_bias)[:, heads],
        "oh_in": onehot,
        "lm_in": linemask,
    }
    arrays = {n: np.ascontiguousarray(v) for n, v in arrays.items()}
    nc = bacc.Bacc("TRN2", target_bir_lowering=False, num_devices=1, dynamic_dma_scratch_size=4096)
    args = [nc.dram_tensor(n, v.shape, F32, kind="ExternalInput").ap() for n, v in arrays.items()]
    out = nc.dram_tensor("out", (P, KC, T), F32, kind="ExternalOutput").ap()
    build(nc, *args, out)
    r = run_bass_kernel_spmd(nc, [arrays], core_ids=[0])
    got = r.results[0]["out"]
    return got.transpose(1, 0, 2).reshape(D, T).T.reshape(1, T, D)
```
